# Optimizing a Trainium2 kernel written in Bass

```python
import math
import jax
import jax.numpy as jnp
from jax import lax
import numpy as np

D_MODEL = 2048
BATCH = 1
SEQ = 512
DEPTH = 1
DEC_BATCH = 8
DEC_SEQ = 1
PAST_LEN = 1024
PAGE_SIZE = 128

HEAD_DIM = 64
N_HEADS = (D_MODEL // 2) // HEAD_DIM
N_KV = N_HEADS // 4
Q_PER_KV = N_HEADS // N_KV
ATTN_W = N_HEADS * HEAD_DIM
KV_W = 2 * N_KV * HEAD_DIM
CMP_BLOCK = 32
CMP_STRIDE = 16
CMP_R = CMP_BLOCK // CMP_STRIDE
CMP_HIDDEN = 2 * HEAD_DIM
SEL_BLOCK = 64
SEL_TOPN = 16
WINDOW = 512
SEL_Q_BLOCK = 64
WIN_Q_BLOCK = 128
SELECT_FORCE = 1.0e4
ATTN_SCALE = HEAD_DIM ** -0.5
D_INNER = D_MODEL // 2
SSM_HEAD_DIM = 64
N_SSM_HEADS = D_INNER // SSM_HEAD_DIM
N_SSM_GROUPS = 2
SSM_HEADS_PER_GROUP = N_SSM_HEADS // N_SSM_GROUPS
D_STATE = 128
CONV_W = 4
CONV_DIM = D_INNER + 2 * N_SSM_GROUPS * D_STATE
SSD_CHUNK = 256
MIX_W = ATTN_W + D_INNER
D_FF = 4 * D_MODEL
IN_SPLITS = (ATTN_W, KV_W, KV_W, KV_W, 3 * N_HEADS, D_INNER, CONV_DIM, N_SSM_HEADS)
IN_COLS = sum(IN_SPLITS)
NORM_EPS = 1e-5

kernel_name = 'nsa_ssd_parallel_hybrid_step'

def rms_norm(x, w):
    xf = x.astype(jnp.float32)
    y = xf * lax.rsqrt(jnp.mean(xf * xf, axis=-1, keepdims=True) + NORM_EPS)
    return (y * w.astype(jnp.float32)).astype(x.dtype)

def masked_softmax(s, mask):
    s = jnp.where(mask, s.astype(jnp.float32), -jnp.inf)
    m = jnp.max(s, axis=-1, keepdims=True)
    m = jnp.where(jnp.isfinite(m), m, 0.0)
    e = jnp.where(mask, jnp.exp(s - m), 0.0)
    return e / jnp.maximum(jnp.sum(e, axis=-1, keepdims=True), 1e-30)

def split_projection(h, w_in):
    B, T, _ = h.shape
    proj = h @ w_in
    parts, off = [], 0
    for width in IN_SPLITS:
        parts.append(proj[..., off:off + width])
        off += width
    q, kc, ks, kw, g, z, xbc, dt_raw = parts
    q = q.reshape(B, T, N_KV, Q_PER_KV, HEAD_DIM)
    kv_shape = (B, T, 2, N_KV, HEAD_DIM)
    gates = jax.nn.sigmoid(g.astype(jnp.float32)).reshape(B, T, N_KV, Q_PER_KV, 3)
    return (q, kc.reshape(kv_shape), ks.reshape(kv_shape), kw.reshape(kv_shape),
            gates, z, xbc, dt_raw)

def compress_kv(kv, pe, w1, b1, w2, b2):
    B, T = kv.shape[:2]
    n_seg = T // CMP_STRIDE
    n_cmp = n_seg - CMP_R + 1
    seg = kv[:, :n_seg * CMP_STRIDE].reshape(B, n_seg, CMP_STRIDE, 2, N_KV, HEAD_DIM)
    w1r = w1.reshape(2, CMP_R, CMP_STRIDE, HEAD_DIM, CMP_HIDDEN)
    proj = jnp.einsum('bsjcgd,crjdf->bsrcgf', seg, w1r)
    hid = sum(proj[:, r:r + n_cmp, r] for r in range(CMP_R))
    pe_term = jnp.einsum('cld,cldf->cf', pe, w1)
    hid = jax.nn.silu(hid + (pe_term + b1)[None, None, :, None, :])
    return jnp.einsum('bncgf,cfd->bncgd', hid, w2) + b2[None, None, :, None, :]

def compressed_attention(q, kc, qpos):
    n_cmp = kc.shape[1]
    s = jnp.einsum('btgrd,bngd->bgrtn', q, kc[:, :, 0]) * ATTN_SCALE
    blk_last = jnp.arange(n_cmp) * CMP_STRIDE + (CMP_BLOCK - 1)
    p = masked_softmax(s, blk_last[None, :] <= qpos[:, None])
    o = jnp.einsum('bgrtn,bngd->btgrd', p, kc[:, :, 1])
    return o.astype(q.dtype), p

def cmp_to_sel_matrix(n_cmp, n_slc):
    ratio = SEL_BLOCK // CMP_STRIDE
    diff = jnp.arange(n_cmp)[:, None] - ratio * jnp.arange(n_slc)[None, :]
    mat = jnp.zeros((n_cmp, n_slc), jnp.float32)
    for n in range(CMP_R):
        mat = mat + ((diff + n >= 0) & (diff + n < ratio)).astype(jnp.float32)
    return mat

def select_blocks(p_cmp, qpos, n_slc):
    imp = jnp.einsum('bgrtn,nj->btgj', p_cmp, cmp_to_sel_matrix(p_cmp.shape[-1], n_slc))
    jt = (qpos // SEL_BLOCK)[:, None]
    j = jnp.arange(n_slc)[None, :]
    forced = (j == 0) | (j == jt) | (j == jt - 1)
    imp = jnp.where(forced[None, :, None, :], SELECT_FORCE, imp)
    imp = jnp.where((j > jt)[None, :, None, :], -SELECT_FORCE, imp)
    _, idx = lax.top_k(imp, min(SEL_TOPN, n_slc))
    return idx

def selected_attention(q, idx, kv, qpos):
    B, T = kv.shape[:2]
    Tq, K = q.shape[1], idx.shape[-1]
    kpos = idx[..., None] * SEL_BLOCK + jnp.arange(SEL_BLOCK)
    bi = jnp.arange(B)[:, None, None, None, None]
    gi = jnp.arange(N_KV)[None, None, :, None, None]
    rows = kv[bi, jnp.minimum(kpos, T - 1), :, gi]
    rows = rows.reshape(B, Tq, N_KV, K * SEL_BLOCK, 2, HEAD_DIM)
    mask = (kpos <= qpos[None, :, None, None, None]).reshape(B, Tq, N_KV, 1, K * SEL_BLOCK)
    s = jnp.einsum('btgrd,btgnd->btgrn', q, rows[..., 0, :]) * ATTN_SCALE
    p = masked_softmax(s, mask)
    return jnp.einsum('btgrn,btgnd->btgrd', p, rows[..., 1, :]).astype(q.dtype)

def window_attention_prompt(q, kv):
    B, T = kv.shape[:2]
    nb, nk = T // WIN_Q_BLOCK, WINDOW // WIN_Q_BLOCK
    kvp = jnp.pad(kv, ((0, 0), (WINDOW, 0), (0, 0), (0, 0), (0, 0)))
    kvp = kvp.reshape(B, nb + nk, WIN_Q_BLOCK, 2, N_KV, HEAD_DIM)
    band = jnp.concatenate([kvp[:, j:j + nb] for j in range(nk + 1)], axis=2)
    qb = q.reshape(B, nb, WIN_Q_BLOCK, N_KV, Q_PER_KV, HEAD_DIM)
    s = jnp.einsum('bnqgrd,bnkgd->bngrqk', qb, band[:, :, :, 0]) * ATTN_SCALE
    start = jnp.arange(nb) * WIN_Q_BLOCK
    qpos = start[:, None] + jnp.arange(WIN_Q_BLOCK)
    kpos = (start - WINDOW)[:, None] + jnp.arange((nk + 1) * WIN_Q_BLOCK)
    d = qpos[:, :, None] - kpos[:, None, :]
    mask = (d >= 0) & (d < WINDOW) & (kpos[:, None, :] >= 0)
    p = masked_softmax(s, mask[None, :, None, None])
    o = jnp.einsum('bngrqk,bnkgd->bnqgrd', p, band[:, :, :, 1])
    return o.reshape(B, T, N_KV, Q_PER_KV, HEAD_DIM).astype(q.dtype)

def window_attention_rows(q, kv, qpos, kpos):
    s = jnp.einsum('btgrd,bkgd->bgrtk', q, kv[:, :, 0]) * ATTN_SCALE
    d = qpos[:, None] - kpos[None, :]
    p = masked_softmax(s, (d >= 0) & (d < WINDOW))
    return jnp.einsum('bgrtk,bkgd->btgrd', p, kv[:, :, 1]).astype(q.dtype)

def gate_branches(gates, o_cmp, o_sel, o_win):
    return gates[..., 0, None] * o_cmp + gates[..., 1, None] * o_sel + gates[..., 2, None] * o_win

def ssd_chunked(x, dt, A, Bm, Cm, s0):
    f32 = jnp.float32
    Bsz, L = x.shape[:2]
    Q = min(SSD_CHUNK, L)
    nc = -(-L // Q)
    pad = nc * Q - L

    def pad_len(a):
        return jnp.pad(a.astype(f32), ((0, 0), (0, pad)) + ((0, 0),) * (a.ndim - 2))

    x, dt, Bm, Cm = pad_len(x), pad_len(dt), pad_len(Bm), pad_len(Cm)
    Gs, Hg = N_SSM_GROUPS, SSM_HEADS_PER_GROUP
    xdt = (x * dt[..., None]).reshape(Bsz, nc, Q, Gs, Hg, SSM_HEAD_DIM)
    a = (dt * A.astype(f32)).reshape(Bsz, nc, Q, Gs, Hg)
    Bc = Bm.reshape(Bsz, nc, Q, Gs, D_STATE)
    Cc = Cm.reshape(Bsz, nc, Q, Gs, D_STATE)
    a_cs = jnp.cumsum(a, axis=2)
    causal = jnp.tril(jnp.ones((Q, Q), bool))[None, None, :, :, None, None]
    seg = a_cs[:, :, :, None] - a_cs[:, :, None, :]
    decay = jnp.exp(jnp.where(causal, seg, -jnp.inf))
    cb = jnp.einsum('bclgn,bcsgn->bclsg', Cc, Bc)
    y_diag = jnp.einsum('bclsg,bclsgh,bcsghp->bclghp', cb, decay, xdt)
    to_end = jnp.exp(a_cs[:, :, -1:] - a_cs)
    chunk_states = jnp.einsum('bcsgn,bcsgh,bcsghp->bcghpn', Bc, to_end, xdt)
    chunk_decay = jnp.exp(a_cs[:, :, -1])

    def carry_step(s, inp):
        st, dc = inp
        return s * dc[..., None, None] + st, s

    s_init = s0.astype(f32).reshape(Bsz, Gs, Hg, SSM_HEAD_DIM, D_STATE)
    s_fin, s_in = lax.scan(carry_step, s_init,
                           (jnp.moveaxis(chunk_states, 1, 0), jnp.moveaxis(chunk_decay, 1, 0)))
    s_in = jnp.moveaxis(s_in, 0, 1)
    y_off = jnp.einsum('bclgn,bcghpn,bclgh->bclghp', Cc, s_in, jnp.exp(a_cs))
    y = (y_diag + y_off).reshape(Bsz, nc * Q, N_SSM_HEADS, SSM_HEAD_DIM)[:, :L]
    return y, s_fin.reshape(Bsz, N_SSM_HEADS, SSM_HEAD_DIM, D_STATE)

def mamba2_mixer(z, xbc, dt_raw, conv_prefix, s0, prm):
    f32 = jnp.float32
    B, L, _ = xbc.shape
    full = jnp.concatenate([conv_prefix.astype(xbc.dtype), xbc], axis=1)
    conv = lax.conv_general_dilated(full, prm['conv_w'][:, None, :].astype(full.dtype),
                                    window_strides=(1,), padding='VALID',
                                    dimension_numbers=('NWC', 'WIO', 'NWC'),
                                    feature_group_count=CONV_DIM)
    act = jax.nn.silu(conv + prm['conv_b'])
    nbc = N_SSM_GROUPS * D_STATE
    xs = act[..., :D_INNER].reshape(B, L, N_SSM_HEADS, SSM_HEAD_DIM)
    Bm = act[..., D_INNER:D_INNER + nbc].reshape(B, L, N_SSM_GROUPS, D_STATE)
    Cm = act[..., D_INNER + nbc:].reshape(B, L, N_SSM_GROUPS, D_STATE)
    dt = jax.nn.softplus(dt_raw.astype(f32) + prm['dt_bias'].astype(f32))
    A = -jnp.exp(prm['a_log'].astype(f32))
    y, s_fin = ssd_chunked(xs, dt, A, Bm, Cm, s0)
    y = y + prm['d_skip'].astype(f32)[:, None] * xs.astype(f32)
    y = y.reshape(B, L, D_INNER) * jax.nn.silu(z.astype(f32))
    yg = y.reshape(B, L, N_SSM_GROUPS, D_INNER // N_SSM_GROUPS)
    yg = yg * lax.rsqrt(jnp.mean(yg * yg, axis=-1, keepdims=True) + NORM_EPS)
    y = yg.reshape(B, L, D_INNER) * prm['ssm_norm'].astype(f32)
    return y.astype(z.dtype), full[:, -(CONV_W - 1):], s_fin

def finish_layer(x, attn, ssd_y, prm):
    B, T, _ = x.shape
    mix = jnp.concatenate([attn.reshape(B, T, ATTN_W).astype(x.dtype), ssd_y], axis=-1) @ prm['w_out']
    x = x + mix
    h = rms_norm(x, prm['ln_mlp'])
    return x + jnp.square(jax.nn.relu(h @ prm['w_up'])) @ prm['w_down']

def cmp_params(prm):
    return prm['cmp_pe'], prm['cmp_w1'], prm['cmp_b1'], prm['cmp_w2'], prm['cmp_b2']

def prompt_layer(x, prm):
    B, T, _ = x.shape
    h = rms_norm(x, prm['ln_mix'])
    q, kv_c, kv_s, kv_w, gates, z, xbc, dt_raw = split_projection(h, prm['w_in'])
    qpos = jnp.arange(T)
    o_cmp, p_cmp = compressed_attention(q, compress_kv(kv_c, *cmp_params(prm)), qpos)
    idx = select_blocks(p_cmp, qpos, -(-T // SEL_BLOCK))
    nb = T // SEL_Q_BLOCK

    def qblocks(a):
        return jnp.moveaxis(a.reshape((B, nb, SEL_Q_BLOCK) + a.shape[2:]), 1, 0)

    o_sel = lax.map(lambda a: selected_attention(a[0], a[1], kv_s, a[2]),
                    (qblocks(q), qblocks(idx), qpos.reshape(nb, SEL_Q_BLOCK)))
    o_sel = jnp.moveaxis(o_sel, 0, 1).reshape(q.shape)
    o_win = window_attention_prompt(q, kv_w)
    attn = gate_branches(gates, o_cmp, o_sel, o_win)
    ssd_y, conv_new, ssm_new = mamba2_mixer(
        z, xbc, dt_raw, jnp.zeros((B, CONV_W - 1, CONV_DIM), xbc.dtype),
        jnp.zeros((B, N_SSM_HEADS, SSM_HEAD_DIM, D_STATE), jnp.float32), prm)
    y = finish_layer(x, attn, ssd_y, prm)
    return y, (kv_c, kv_s, kv_w[:, -min(WINDOW, T):], conv_new, ssm_new.astype(x.dtype))

def sample_layer(x, cache_c, cache_s, win_buf, conv_st, ssm_st, page_table, prm):
    B, T, _ = x.shape
    past = page_table.shape[1] * cache_c.shape[1]
    h = rms_norm(x, prm['ln_mix'])
    q, kv_c, kv_s, kv_w, gates, z, xbc, dt_raw = split_projection(h, prm['w_in'])
    qpos = past + jnp.arange(T)

    def paged_rows(cache):
        return cache[page_table].reshape((B, past) + cache.shape[2:]).astype(x.dtype)

    full_c = jnp.concatenate([paged_rows(cache_c), kv_c], axis=1)
    full_s = jnp.concatenate([paged_rows(cache_s), kv_s], axis=1)
    o_cmp, p_cmp = compressed_attention(q, compress_kv(full_c, *cmp_params(prm)), qpos)
    idx = select_blocks(p_cmp, qpos, -(-(past + T) // SEL_BLOCK))
    o_sel = selected_attention(q, idx, full_s, qpos)
    n_buf = win_buf.shape[1]
    win_rows = jnp.concatenate([win_buf.astype(x.dtype), kv_w], axis=1)
    kpos = past - n_buf + jnp.arange(n_buf + T)
    o_win = window_attention_rows(q, win_rows, qpos, kpos)
    attn = gate_branches(gates, o_cmp, o_sel, o_win)
    ssd_y, conv_new, ssm_new = mamba2_mixer(z, xbc, dt_raw, conv_st, ssm_st, prm)
    y = finish_layer(x, attn, ssd_y, prm)
    return y, (kv_c, kv_s, win_rows[:, -min(WINDOW, past + T):], conv_new,
               ssm_new.astype(ssm_st.dtype))

def setup_inputs(seed: int = 0) -> dict:
    key = jax.random.key(seed)
    ks = jax.random.split(key, 32)
    f32 = jnp.float32

    def nrm(k, shape, scale):
        return scale * jax.random.normal(k, shape, f32)

    n_pages = PAST_LEN // PAGE_SIZE
    n_pool = (DEC_BATCH * n_pages * 5) // 4
    w_buf = min(WINDOW, PAST_LEN)
    page_table = jax.random.permutation(ks[0], n_pool)[:DEC_BATCH * n_pages]
    page_table = page_table.reshape(DEC_BATCH, n_pages).astype(jnp.int32)
    dt0 = jnp.exp(jax.random.uniform(ks[1], (DEPTH, N_SSM_HEADS), f32,
                                     math.log(1e-3), math.log(1e-1)))
    return {
        'x_prompt': nrm(ks[2], (BATCH, SEQ, D_MODEL), 1.0),
        'x_sample': nrm(ks[3], (DEC_BATCH, DEC_SEQ, D_MODEL), 1.0),
        'cache_kv_cmp': nrm(ks[4], (DEPTH, n_pool, PAGE_SIZE, 2, N_KV, HEAD_DIM), 1.0),
        'cache_kv_sel': nrm(ks[5], (DEPTH, n_pool, PAGE_SIZE, 2, N_KV, HEAD_DIM), 1.0),
        'state_kv_win': nrm(ks[6], (DEPTH, DEC_BATCH, w_buf, 2, N_KV, HEAD_DIM), 1.0),
        'state_conv': nrm(ks[7], (DEPTH, DEC_BATCH, CONV_W - 1, CONV_DIM), 1.0),
        'state_ssm': nrm(ks[8], (DEPTH, DEC_BATCH, N_SSM_HEADS, SSM_HEAD_DIM, D_STATE), 0.1),
        'page_table': page_table,
        'ln_mix': 1.0 + nrm(ks[9], (DEPTH, D_MODEL), 0.02),
        'w_in': nrm(ks[10], (DEPTH, D_MODEL, IN_COLS), D_MODEL ** -0.5),
        'cmp_pe': nrm(ks[11], (DEPTH, 2, CMP_BLOCK, HEAD_DIM), 0.1),
        'cmp_w1': nrm(ks[12], (DEPTH, 2, CMP_BLOCK, HEAD_DIM, CMP_HIDDEN), (CMP_BLOCK * HEAD_DIM) ** -0.5),
        'cmp_b1': nrm(ks[13], (DEPTH, 2, CMP_HIDDEN), 0.02),
        'cmp_w2': nrm(ks[14], (DEPTH, 2, CMP_HIDDEN, HEAD_DIM), CMP_HIDDEN ** -0.5),
        'cmp_b2': nrm(ks[15], (DEPTH, 2, HEAD_DIM), 0.02),
        'conv_w': nrm(ks[16], (DEPTH, CONV_W, CONV_DIM), CONV_W ** -0.5),
        'conv_b': nrm(ks[17], (DEPTH, CONV_DIM), 0.02),
        'dt_bias': dt0 + jnp.log(-jnp.expm1(-dt0)),
        'a_log': jnp.log(jax.random.uniform(ks[18], (DEPTH, N_SSM_HEADS), f32, 1.0, 16.0)),
        'd_skip': 1.0 + nrm(ks[19], (DEPTH, N_SSM_HEADS), 0.1),
        'ssm_norm': 1.0 + nrm(ks[20], (DEPTH, D_INNER), 0.02),
        'w_out': nrm(ks[21], (DEPTH, MIX_W, D_MODEL), MIX_W ** -0.5),
        'ln_mlp': 1.0 + nrm(ks[22], (DEPTH, D_MODEL), 0.02),
        'w_up': nrm(ks[23], (DEPTH, D_MODEL, D_FF), D_MODEL ** -0.5),
        'w_down': nrm(ks[24], (DEPTH, D_FF, D_MODEL), D_FF ** -0.5),
        'ln_final': 1.0 + nrm(ks[25], (D_MODEL,), 0.02),
    }

def reference(x_prompt, x_sample, cache_kv_cmp, cache_kv_sel, state_kv_win, state_conv,
              state_ssm, page_table, ln_mix, w_in, cmp_pe, cmp_w1, cmp_b1, cmp_w2, cmp_b2,
              conv_w, conv_b, dt_bias, a_log, d_skip, ssm_norm, w_out, ln_mlp, w_up, w_down,
              ln_final):
    hp, hs = x_prompt, x_sample
    new_p, new_s = [], []
    for l in range(DEPTH):
        prm = {'ln_mix': ln_mix[l], 'w_in': w_in[l], 'cmp_pe': cmp_pe[l], 'cmp_w1': cmp_w1[l],
               'cmp_b1': cmp_b1[l], 'cmp_w2': cmp_w2[l], 'cmp_b2': cmp_b2[l],
               'conv_w': conv_w[l], 'conv_b': conv_b[l], 'dt_bias': dt_bias[l],
               'a_log': a_log[l], 'd_skip': d_skip[l], 'ssm_norm': ssm_norm[l],
               'w_out': w_out[l], 'ln_mlp': ln_mlp[l], 'w_up': w_up[l], 'w_down': w_down[l]}
        hp, st_p = prompt_layer(hp, prm)
        hs, st_s = sample_layer(hs, cache_kv_cmp[l], cache_kv_sel[l], state_kv_win[l],
                                state_conv[l], state_ssm[l], page_table, prm)
        new_p.append(st_p)
        new_s.append(st_s)
    y_prompt = rms_norm(hp, ln_final)
    y_sample = rms_norm(hs, ln_final)
    kv_cmp_p = jnp.stack([s[0] for s in new_p])
    kv_sel_p = jnp.stack([s[1] for s in new_p])
    kv_win_p = jnp.stack([s[2] for s in new_p])
    conv_p = jnp.stack([s[3] for s in new_p])
    ssm_p = jnp.stack([s[4] for s in new_p])
    kv_cmp_s = jnp.stack([s[0] for s in new_s])
    kv_sel_s = jnp.stack([s[1] for s in new_s])
    kv_win_s = jnp.stack([s[2] for s in new_s])
    conv_s = jnp.stack([s[3] for s in new_s])
    ssm_s = jnp.stack([s[4] for s in new_s])
    return (y_prompt, y_sample, kv_cmp_p, kv_sel_p, kv_win_p, conv_p, ssm_p,
            kv_cmp_s, kv_sel_s, kv_win_s, conv_s, ssm_s)


_drawn_inputs = setup_inputs


def setup_inputs(seed=0):
    import zlib

    import numpy as np

    out = dict(_drawn_inputs(seed))
    spreads = {}
    factors = {'cache_kv_sel': 3.387,
     'cmp_pe': 21.533,
     'cmp_b1': 77.059,
     'cmp_b2': 22.329,
     'ssm_norm': 12.636,
     'ln_mlp': 9.963,
     'ln_final': 20.204,
     'cache_kv_cmp': 5.06,
     'cmp_w1': 3.167}
    for name, (base, spread) in spreads.items():
        noise = np.random.default_rng([zlib.crc32(name.encode()), seed]).standard_normal(out[name].shape)
        drawn = base * np.exp(spread * noise) if base else spread * noise
        out[name] = jnp.asarray(drawn.astype(out[name].dtype))
    for name, factor in factors.items():
        out[name] = (out[name] * factor).astype(out[name].dtype)
    return out
```

```python
from contextlib import ExitStack

import concourse.bass as bass
from concourse import mybir

F32 = mybir.dt.float32
F32R = mybir.dt.float32r
I32 = mybir.dt.int32
U32 = mybir.dt.uint32
ALU = mybir.AluOpType
ACT = mybir.ActivationFunctionType
AX = mybir.AxisListType

P = 128
D_MODEL = 2048
SEQ = 512
NB = 8
NT = SEQ + NB
HN = NT // 2
KT = D_MODEL // P
PAST = 1024
PAGE = 128
N_PAGES = PAST // PAGE
N_POOL = NB * N_PAGES * 5 // 4
HD = 64
NH = 16
NKV = 4
RPG = NH // NKV
KVW = 2 * NKV * HD
CHID = 2 * HD
STRIDE = 16
NCMP_S = PAST // STRIDE - 1
NCMP_P = SEQ // STRIDE - 1
WIN = 512
DI = 1024
NG = 2
DS = 128
CONV_DIM = DI + 2 * NG * DS
MIX = 2048
DFF = 4 * D_MODEL
EPS = 1e-5
NEG = -1.0e30

C_Q, C_KV, C_GATE, C_Z, C_DT = 0, 1024, 1024 + 3 * KVW, 1024 + 3 * KVW + 48, 1024 + 3 * KVW + 48 + 1024 + CONV_DIM
IN_COLS = C_DT + NH
T_Q, T_KC, T_KS, T_KW, T_Z, T_X, T_GD = 0, 8, 12, 16, 20, 28, 40
NTILE = 41
DT0 = 64

PK, PN = 4, 256
N_RAW, N_SPLIT = 4, 2
IN_BLOCKS = 20
Q_PIECES = 16
IN_PIECES = IN_BLOCKS * (KT // PK)
GD_PIECES = KT // PK
OUT_BLOCKS = D_MODEL // PN
OUT_PIECES = OUT_BLOCKS * (MIX // P // PK)
FC = 1024
N_CHUNK = DFF // FC
UP_BLOCKS, DOWN_BLOCKS = FC // PN, D_MODEL // PN
UP_PIECES, DOWN_PIECES = UP_BLOCKS * (KT // PK), DOWN_BLOCKS * (FC // P // PK)
CHUNK_PIECES = UP_PIECES + DOWN_PIECES
OUT0 = IN_PIECES + GD_PIECES
MLP0 = OUT0 + OUT_PIECES

R_LNMIX, R_LNMLP, R_LNFIN, R_SSMN, R_CB, R_CW, R_B1, R_B2K = 0, 16, 32, 48, 56, 68, 116, 118


class Chain:

    def __init__(self, eng, sem):
        self.eng, self.sem, self.n = eng, sem, 0

    def step(self, ins):
        self.n += 1
        ins.then_inc(self.sem, 1)
        return ins

    def settle(self):
        self.eng.wait_ge(self.sem, self.n)


class Part:

    def __init__(self, sem, base):
        self.sem, self.base = sem, base

    def __call__(self, n):
        return self.sem, n + self.base


def build_program(nc, i, o):
    with ExitStack() as ctx:
        def sem(name):
            return ctx.enter_context(nc.semaphore(name))

        def series(name, *parts):
            shared, base_ = sem(name), 0
            for _, count in parts:
                yield Part(shared, base_)
                base_ += count

        x_hi, x_sq, x_rms = series(
            "x_act_done", ("x_hi", 16), ("x_sq", 1), ("x_rms", 1))
        x_lo, x_diag = series(
            "x_dve_done", ("x_lo", 16), ("x_diag", 5))
        x_turned, x_bcd = series(
            "x_pe_done", ("x_turned", 16), ("x_bcd", 1))
        p_turned, p_prod, p_w2 = series(
            "p_pe_done", ("p_turned", 8), ("p_prod", 4), ("p_w2", 2))
        p_order, p_ev, p_sum, p_out = series(
            "p_dve_done", ("p_order", 1), ("p_ev", 8), ("p_sum", 2), ("p_out", 3))
        p_half, p_silu = series(
            "p_act_done", ("p_half", 2), ("p_silu", 2))
        a_gate, a_mask = series(
            "a_act_done", ("a_gate", 2), ("a_mask", 2))
        n_q, nc_max, nc_p, nc_Tc, n_imp1, n_drop = series(
            "n_dve_first", ("n_q", 1), ("nc_max", 1), ("nc_p", 2), ("nc_Tc", 2), ("n_imp1", 1), ("n_drop", 1))
        nc_s, nc_T, n_imp = series(
            "n_pe_first", ("nc_s", 1), ("nc_T", 1), ("n_imp", 2))
        n_max, n_pd = series(
            "n_dve_last", ("n_max", 2), ("n_pd", 3))
        n_oc, n_o, n_mix = series(
            "n_dve_end", ("n_oc", 4), ("n_o", 2), ("n_mix", 8))
        d_u, d_ln, e_dd, d_xa, f_z, d_te, d_btok = series(
            "d_act_done", ("d_u", 1), ("d_ln", 2), ("e_dd", 1), ("d_xa", 12), ("f_z", 8), ("d_te", 2), ("d_btok", 2))
        d_xp, d_e, d_acs, d_diag, d_conv, d_dta, d_ae, d_xdt, d_cbm = series(
            "d_dve_done", ("d_xp", 1), ("d_e", 2), ("d_acs", 4), ("d_diag", 4), ("d_conv", 12), ("d_dta", 1), ("d_ae", 1),
            ("d_xdt", 8), ("d_cbm", 2))
        d_ct, d_T, d_xT, d_bT, d_cb, d_st = series(
            "d_pe_done", ("d_ct", 1), ("d_T", 2), ("d_xT", 8), ("d_bT", 2), ("d_cb", 2), ("d_st", 8))
        f_so, f_sq, f_rms = series(
            "f_act_done", ("f_so", 2), ("f_sq", 8), ("f_rms", 2))
        f_T, f_sum = series(
            "f_pe_done", ("f_T", 2), ("f_sum", 8))
        f_g, f_mix = series(
            "f_dve_done", ("f_g", 8), ("f_mix", 8))
        arena = ctx.enter_context(nc.sbuf_tensor("arena", [P, 53200], F32))
        base = nc.sbuf_base - 53200 * 4
        limit = 53200 * 4

        def at(name, shape, off, dt=F32):
            n = 4
            for s in shape[1:]:
                n *= s
            assert off + n <= limit, (name, off + n, limit)
            return nc.alloc_sbuf_tensor_at(name, shape, dt, offset=base + off)

        TILE = NT * 4
        M_CONST, M_RING = 0, 12288
        M_RAW, M_HI, M_LO = M_RING, M_RING + 16384, M_RING + 24576
        M0 = M_RING + 32768
        A0, A1, A2, A3, A4 = (M0 + n * KT * TILE for n in range(5))
        MF = A2 + NTILE * TILE

        ident = at("ident", [P, P], 0)
        ones = at("ones", [P, P], 512)
        pcol = at("pcol", [P, P], 1024)
        rstd_bc = at("rstd_bc", [P, 2, HN], 1536)
        small = at("small", [P, 64], 1536 + TILE)
        idx_c = at("idx_c", [P, 4], 3872, U32)
        idx_s = at("idx_s", [P, NB], 3904, U32)
        kc_T = at("kc_T", [P, 2, NB, 64], 4096)
        kcp_T = at("kcp_T", [P, 2, 32], 8192)
        bias1 = at("bias1", [P, 2], 8448)
        w_raw = at("w_raw", [P, N_RAW, PK, PN], M_RAW)
        w_hi = at("w_hi", [P, N_SPLIT, PK, PN], M_HI, F32R)
        w_lo = at("w_lo", [P, N_SPLIT, PK, PN], M_LO, F32R)
        h_hi = at("h_hi", [P, KT, NT], A0, F32R)
        h_lo = at("h_lo", [P, KT, NT], A1, F32R)
        proj = at("proj", [P, NTILE, 2, HN], A2)
        pt = proj[:].rearrange("p t h n -> p t (h n)")
        vc = at("vc", [64, NB, 256], MF)
        vcp = at("vcp", [32, 256], MF + 8192)
        seg_raw = at("seg_raw", [P, STRIDE, 8, HD], A0)
        seg_ord = at("seg_ord", [P, 8, STRIDE, HD], A0 + 32768)
        segT = at("segT", [P, 2, 8, 8, P], A2)
        w1 = at("w1", [P, 2, 2, 8, CHID], A2 + 65536)
        xtok = at("xtok", [P, 4, D_MODEL], A2)
        xs_tok = at("xs_tok", [NB, D_MODEL], M_LO)
        sq_junk = at("sq_junk", [P, D_MODEL], A2 + 40960)

        PS = ctx.enter_context(nc.psum_tensor("PS", [P, 8, 512], F32))
        psf = PS[:].rearrange("p b n -> p (b n)")

        block = ctx.enter_context(nc.Block())

        cmask = at("cmask", [P, P], 8704)
        causT = at("causT", [P, P], 9216)
        b2v_bc = at("b2v_bc", [P, HD], 9728)
        cmpmask = at("cmpmask", [P, 4, 32], 9984)
        same_grp = at("same_grp", [P, P], 10496)
        sel_mat = at("sel_mat", [64, 17], 11008)
        own_batch = at("own_batch", [P, NB], 11104)
        dskip = at("dskip", [P, 8], 11136)
        hpar = at("hpar", [P, 4], 11168)
        blk_no = at("blk_no", [P, 17], 11200)
        valid0 = at("valid0", [P, 1], 11296)
        eps_col = at("eps_col", [P, 1], 11328)
        blk_i = at("blk_i", [P, 17], 11360, I32)
        pidx = at("pidx", [P, 4], 11456, I32)
        ptab_c = at("ptab_c", [P, 4], 11488, I32)
        ptab_s = at("ptab_s", [P, NB], 11520, I32)
        sel_m2 = at("sel_m2", [64, 17], 11552)
        prow = at("prow", [P, P], MF + 9984)
        pe_row = at("pe_row", [32, P], MF + 10496)
        peT = at("peT", [P, 32], MF + 11008)
        w2 = at("w2", [P, 2, HD], MF + 11136)

        small_ld, pool_c, pe_par, par_c = sem("small_ld"), sem("pool_c"), sem("pe_par"), sem("par_c")
        dve_ch, act_ch, pool_ch = sem("dve_ch"), sem("act_ch"), sem("pool_ch")
        w1_ld, tab_ld, idx_rdy = sem("w1_ld"), sem("tab_ld"), sem("idx_rdy")

        SMALL_LOADS = []

        def rows(src, lo, n):
            SMALL_LOADS.append((prow[lo:lo + n, :], src))

        one = lambda ap: ap.rearrange("a (k p) -> (a k) p", p=P)
        rows(one(i["ln_mix"]), R_LNMIX, 16)
        rows(one(i["ln_mlp"]), R_LNMLP, 16)
        rows(i["ln_final"].rearrange("(k p) -> k p", p=P), R_LNFIN, 16)
        rows(one(i["ssm_norm"]), R_SSMN, 8)
        rows(one(i["conv_b"]), R_CB, 12)
        rows(i["conv_w"].rearrange("a w (k p) -> (a w k) p", p=P), R_CW, 48)
        rows(i["cmp_b1"].rearrange("a c f -> (a c) f"), R_B1, 2)
        for half in range(2):
            SMALL_LOADS.append((prow[R_B2K:R_B2K + 1, half * HD:half * HD + HD], i["cmp_b2"][0, 0:1, :]))
        SMALL_LOADS.append((pe_row[:], i["cmp_pe"].rearrange("a c (l j) d -> (a c l) (j d)", j=2)))
        SMALL_LOADS.append((w2[:], i["cmp_w2"].rearrange("a c f d -> f (a c) d")))
        SMALL_LOADS.append((b2v_bc[:], i["cmp_b2"][0, 1, :].partition_broadcast(P)))
        SMALL_LOADS.append((hpar[DT0:DT0 + NH, 0:1], i["dt_bias"].rearrange("a h -> h a")))
        SMALL_LOADS.append((hpar[DT0:DT0 + NH, 1:2], i["a_log"].rearrange("a h -> h a")))
        for half in range(2):
            SMALL_LOADS.append((dskip[half * HD:half * HD + HD, :],
                                i["d_skip"].rearrange("a (k h) -> (a h) k", h=2)[half].partition_broadcast(HD)))
        N_SMALL = len(SMALL_LOADS)

        def const_sp(e):
            pg = i["page_table"]
            for s in range(4):
                e.dma_start(ptab_c[:, s:s + 1], bass.AP(pg.tensor, 16 * s, [[1, 16], [0, 8]]),
                            allow_slow_non_contiguous=True).then_inc(tab_ld, 16)
            for b in range(NB):
                e.dma_start(ptab_s[:, b:b + 1], bass.AP(pg.tensor, 8 * b, [[1, 8], [0, 16]]),
                            allow_slow_non_contiguous=True).then_inc(tab_ld, 16)
            e.wait_ge(pool_c, 1)
            for dst, src in SMALL_LOADS:
                e.dma_start(dst, src, allow_slow_non_contiguous=True).then_inc(small_ld, 16)
            e.wait_ge(seg_ld, 16)
            e.dma_start(w1[:].rearrange("p c r j f -> p c (r j) f"),
                        i["cmp_w1"].rearrange("a c (l j) d f -> (a j d) c l f", j=2)).then_inc(w1_ld, 16)

        def const_pool(e, ch):
            def keep(tile, op, fill, base_, cm, pattern):
                ch.settle()
                ch.step(e.affine_select(out=tile, in_=tile, compare_op=op, fill=fill, base=base_,
                                        pattern=pattern, channel_multiplier=cm))
            e.memset(prow[:], 0.0).then_inc(pool_c, 1)
            ch.step(e.iota(pidx[:, 0:1], pattern=[[0, 1]], base=0, channel_multiplier=1))
            ch.step(e.memset(ident[:], 0.0))
            keep(ident[:], ALU.not_equal, 1.0, 0, 1, [[-1, P]])
            ch.settle()
            e.memset(ones[:], 1.0).then_inc(pool_c, 1)

        def const2_pool(e, ch):
            def keep(tile, op, fill, base_, cm, pattern):
                ch.settle()
                ch.step(e.affine_select(out=tile, in_=tile, compare_op=op, fill=fill, base=base_,
                                        pattern=pattern, channel_multiplier=cm))
            for tile, v in ((cmask, 0.0), (causT, 1.0), (cmpmask, 0.0), (same_grp, 1.0), (sel_mat, 1.0),
                            (sel_m2, 1.0), (own_batch, 1.0), (valid0, 1.0), (small, 1.0), (eps_col, EPS)):
                ch.step(e.memset(tile[:], v))
            ch.step(e.iota(blk_i[:], pattern=[[1, 17]], base=1, channel_multiplier=0))
            keep(cmask[:], ALU.is_ge, NEG, 0, 1, [[-1, P]])
            keep(causT[:], ALU.is_ge, 0.0, 0, -1, [[1, P]])
            keep(cmpmask[:], ALU.is_ge, NEG, -(2 * STRIDE - 1), 1, [[P, 4], [-STRIDE, 32]])
            keep(same_grp[:], ALU.is_ge, 0.0, 0, 1, [[-4, 32], [0, 4]])
            keep(same_grp[:], ALU.is_ge, 0.0, 3, -1, [[4, 32], [0, 4]])
            keep(own_batch[:], ALU.is_ge, 0.0, 0, 1, [[-NH, NB]])
            keep(own_batch[:], ALU.is_ge, 0.0, NH - 1, -1, [[NH, NB]])
            keep(sel_mat[:], ALU.is_ge, 0.0, 0, 1, [[-4, 17]])
            keep(sel_mat[:], ALU.is_ge, 0.0, 3, -1, [[4, 17]])
            keep(sel_m2[:], ALU.is_ge, 0.0, 1, 1, [[-4, 17]])
            keep(sel_m2[:], ALU.is_ge, 0.0, 2, -1, [[4, 17]])
            keep(valid0[:], ALU.is_ge, 0.0, -(2 * STRIDE - 1), 1, [[0, 1]])
            ch.settle()
            ch.step(e.tensor_tensor(sel_mat[:], sel_mat[:], sel_m2[:], ALU.add))
            ch.step(e.tensor_copy(blk_no[:], blk_i[:]))
            ch.settle()
            e.memset(kcp_T[:], 0.0).then_inc(pool_c, 1)

        def const_dve(e, ch):
            e.wait_ge(pool_c, 2)
            ch.step(e.tensor_scalar(pidx[:, 1:2], pidx[:, 0:1], 7, None, ALU.bitwise_and))
            ch.step(e.tensor_scalar(pidx[:, 2:3], pidx[:, 0:1], 15, None, ALU.bitwise_and))
            ch.settle()
            e.wait_ge(tab_ld, 16 * 12)
            for s in range(4):
                e.scalar_tensor_tensor(out=idx_c[:, s:s + 1], in0=ptab_c[:, s:s + 1], scalar=8.0,
                                       in1=pidx[:, 1:2], op0=ALU.mult, op1=ALU.add).then_inc(idx_rdy, 1)
            for b in range(NB):
                e.scalar_tensor_tensor(out=idx_s[:, b:b + 1], in0=ptab_s[:, b:b + 1], scalar=16.0,
                                       in1=pidx[:, 2:3], op0=ALU.mult, op1=ALU.add).then_inc(idx_rdy, 1)
            e.wait_ge(pe_par, 2)
            ch.step(e.tensor_copy(pcol[:], PS[:, 0, 0:P]))
            e.tensor_copy(peT[:], PS[:, 1, 0:32]).then_inc(par_c, 1)
            ch.settle()

        def bias_dve(e):
            e.wait_ge(pe_par, 3)
            e.tensor_tensor(bias1[:], PS[:, 4, 0:2], pcol[:, R_B1:R_B1 + 2], ALU.add).then_inc(par_c, 1)

        def const_pe(e):
            e.wait_ge(pool_c, 2)
            e.wait_ge(small_ld, 16 * N_SMALL)
            e.transpose(PS[:, 0, 0:P], prow[:], ident[:]).then_inc(pe_par, 1)
            e.transpose(PS[:, 1, 0:32], pe_row[:], ident[0:32, 0:32]).then_inc(pe_par, 1)

        def bias_pe(e):
            e.wait_ge(w1_ld, 16)
            for c in range(2):
                for l in range(16):
                    last = e.matmul(PS[:, 4, c:c + 1], w1[:, c, l // 8, l % 8, :], peT[:, c * 16 + l:c * 16 + l + 1],
                                    start=(l == 0), stop=(l == 15))
            last.then_inc(pe_par, 1)

        N_ST = 4
        seg_ld, c_order = sem("seg_ld"), sem("c_order")
        c_turned, c_ev_act, c_ev_dve = sem("c_turned"), sem("c_ev_act"), sem("c_ev_dve")
        c_prod, c_half, c_sum, c_silu, c_w2, c_kout, c_vout = (
            sem(n) for n in ("c_prod", "c_half", "c_sum", "c_silu", "c_w2", "c_kout", "c_vout"))
        second = at("second", [P, 2, 8, 64], MF + 11648)
        assert MF + 11648 + 4096 <= limit
        hid = at("hid", [P, 2, 8, 64], M_HI + 4096)
        hid_s = at("hid_s", [P, 2, 8, 64], M_HI)

        def compress_pool(e):
            rows_c = i["cache_kv_cmp"].rearrange("a n (s j) c g d -> (a n s) (j c g d)", j=STRIDE)
            for t in range(N_ST):
                if t == 0:
                    e.wait_ge(idx_rdy, 4)
                else:
                    e.wait_ge(c_order, 8 * t)
                e.indirect_dma_start(
                    out=seg_raw[:].rearrange("p j c d -> p (j c d)"), out_offset=None, in_=rows_c,
                    in_offset=bass.IndirectOffsetOnAxis(ap=idx_c[:, t:t + 1], axis=0)).then_inc(seg_ld, 16)

        def compress_pe(e):
            e.wait_ge(par_c, 1)
            def turn(t):
                for cg in range(8):
                    e.wait_ge(c_order, 8 * t + cg + 1)
                    for h in range(2):
                        f = (t * 8 + cg) * 2 + h
                        if f >= 4:
                            e.wait_ge((c_ev_act, c_ev_dve)[h], f // 2 - 1)
                        for x in range(4):
                            j = 2 * (4 * h + x)
                            last = e.transpose(PS[:, f % 4, x * P:x * P + P],
                                               seg_ord[:, cg, j:j + 2, :].rearrange("p j d -> p (j d)"), ident[:])
                        last.then_inc(c_turned, 1)

            def products(t):
                e.wait_ge(c_ev_act, 8 * (t + 1))
                e.wait_ge(c_ev_dve, 8 * (t + 1))
                for r in (1, 0):
                    for c in range(2):
                        if t and r == 1:
                            e.wait_ge(c_half, 2 * t)
                        elif t:
                            e.wait_ge((c_kout, c_vout)[c], t)
                        for j in range(8):
                            last = e.matmul(PS[:, 4 + 2 * c + r, :], w1[:, c, r, j, :],
                                            segT[:, t % 2, 4 * c:4 * c + 4, j, :],
                                            start=(j == 0), stop=(j == 7))
                        last.then_inc(c_prod, 1)

            def second_layer(t):
                e.wait_ge(c_silu, 2 * t + 1)
                for g in range(NKV):
                    last = e.matmul(PS[(g % 2) * HD:(g % 2) * HD + HD, 4, (g // 2) * P:(g // 2) * P + P]
                                    .rearrange("p (b n) -> p b n", b=2)[:, :, 0:NCMP_S],
                                    w2[:, 0, :], hid_s[:, 0, 2 * g:2 * g + 2, 0:NCMP_S], start=True, stop=True)
                last.then_inc(c_w2, 1)
                e.wait_ge(c_silu, 2 * t + 2)
                for b in range(2):
                    for g in range(NKV):
                        last = e.matmul(PS[0:NCMP_S, 6, (b * 4 + g) * HD:(b * 4 + g) * HD + HD],
                                        hid_s[:, 1, 2 * g + b, 0:NCMP_S], w2[:, 1, :], start=True, stop=True)
                last.then_inc(c_w2, 1)

            turn(0)
            bias_pe(e)
            for t in range(N_ST):
                if t + 1 < N_ST:
                    turn(t + 1)
                if t == 0:
                    e.wait_ge(par_c, 2)
                if t:
                    second_layer(t - 1)
                products(t)
            second_layer(N_ST - 1)

        def turned_copy(t, h, copy, done, e):
            if t >= 2:
                e.wait_ge(c_prod, 4 * (t - 1))
            for cg in range(8):
                f = (t * 8 + cg) * 2 + h
                e.wait_ge(c_turned, f + 1)
                copy(segT[:, t % 2, cg, 4 * h:4 * h + 4, :],
                     PS[:, f % 4, :].rearrange("p (j s) -> p j s", j=4)).then_inc(done, 1)

        def compress_act(e):
            copy = lambda out, in_: e.activation(out, in_, ACT.Copy)
            turned_copy(0, 0, copy, c_ev_act, e)
            for t in range(N_ST):
                if t + 1 < N_ST:
                    turned_copy(t + 1, 0, copy, c_ev_act, e)
                for c in range(2):
                    e.wait_ge(c_prod, 4 * t + c + 1)
                    if t:
                        e.wait_ge(c_sum, 2 * t)
                    copy(second[:, c].rearrange("p g n -> p (g n)"), PS[:, 5 + 2 * c, :]).then_inc(c_half, 1)
                e.wait_ge(par_c, 2)
                for c in range(2):
                    e.wait_ge(c_sum, 2 * t + c + 1)
                    if t:
                        e.wait_ge(c_w2, 2 * t)
                    e.activation(hid_s[:, c, :, 0:NCMP_S], hid[:, c, :, 0:NCMP_S], ACT.Silu,
                                 bias=bias1[:, c:c + 1]).then_inc(c_silu, 1)

        def compress_dve(e):
            def outputs(t):
                e.wait_ge(c_w2, 2 * t + 1)
                for gp in range(2):
                    last = e.tensor_scalar(kc_T[:, gp, 2 * t:2 * t + 2, 0:NCMP_S],
                                           PS[:, 4, gp * P:gp * P + P].rearrange("p (b n) -> p b n", b=2)[:, :, 0:NCMP_S],
                                           pcol[:, R_B2K:R_B2K + 1], None, ALU.add)
                last.then_inc(c_kout, 1)
                e.wait_ge(c_w2, 2 * t + 2)
                e.tensor_tensor(vc[0:NCMP_S, 2 * t:2 * t + 2, :].rearrange("p b (g d) -> p (b g) d", d=HD),
                                PS[0:NCMP_S, 6, :].rearrange("p (x d) -> p x d", d=HD),
                                b2v_bc[0:NCMP_S, :].unsqueeze(1).to_broadcast([NCMP_S, 8, HD]),
                                ALU.add).then_inc(c_vout, 1)

            copy = lambda out, in_: e.tensor_copy(out, in_)

            def order(t):
                e.wait_ge(seg_ld, 16 * (t + 1))
                for cg in range(8):
                    if t:
                        e.wait_ge(c_turned, 16 * (t - 1) + 2 * cg + 2)
                    e.tensor_copy(seg_ord[:, cg], seg_raw[:, :, cg, :]).then_inc(c_order, 1)
            order(0)
            turned_copy(0, 1, copy, c_ev_dve, e)
            bias_dve(e)
            for t in range(N_ST):
                if t + 1 < N_ST:
                    order(t + 1)
                    turned_copy(t + 1, 1, copy, c_ev_dve, e)
                if t:
                    outputs(t - 1)
                for c in range(2):
                    e.wait_ge(c_prod, 4 * t + 3 + c)
                    e.wait_ge(c_half, 2 * t + 1 + c)
                    if t:
                        e.wait_ge(c_silu, 2 * t)
                    e.tensor_tensor(hid[:, c, :, 0:NCMP_S],
                                    PS[:, 4 + 2 * c, :].rearrange("p (g n) -> p g n", n=64)[:, :, 0:NCMP_S],
                                    second[:, c, :, 1:64], ALU.add).then_inc(c_sum, 1)
            outputs(N_ST - 1)

        xs_ld = [sem(f"xs_ld{n}") for n in range(5)]
        diag = at("diag", [P, 4, P], A2 + 49152)
        diag_s = at("diag_s", [NB, NB], A2 + 51200)
        ssq, rms, rstd = small[:, 0:5], small[:, 8:13], small[:, 16:21]

        def x_sp(e):
            e.wait_ge(c_prod, 4 * (N_ST - 1))
            for t in range(4):
                e.dma_start(xtok[:, t, :], i["x_prompt"][0, t * P:t * P + P, :]).then_inc(xs_ld[t], 16)
            e.dma_start(xs_tok[:], i["x_sample"].rearrange("b t d -> (b t) d")).then_inc(xs_ld[4], 16)

        def x_act(e, ch):
            e.wait_ge(pool_c, 3)
            for k in range(KT):
                e.wait_ge(*x_turned(k + 1))
                s = 2 * (k % 3)
                e.activation(h_hi[:, k, :], psf[:, s * 512:s * 512 + NT], ACT.Copy,
                             scale=pcol[:, R_LNMIX + k:R_LNMIX + k + 1]).then_inc(x_hi.sem, 1)
            square_sum(e, ch, 4)

        def square_sum(e, ch, t):
            e.wait_ge(xs_ld[t], 16)
            src = xtok[:, t, :] if t < 4 else xs_tok[:]
            n = P if t < 4 else NB
            if ch.n:
                ch.settle()
            ch.step(e.activation(sq_junk[0:n, :], src, ACT.Square, accum_out=ssq[0:n, t:t + 1]))

        def token_rms(e, ch):
            ch.settle()
            e.activation(rms, ssq, ACT.Sqrt, scale=1.0 / D_MODEL, bias=eps_col[:]).then_inc(x_sq.sem, 1)
            e.wait_ge(*x_bcd(1))
            rf = rstd_bc[:].rearrange("p h n -> p (h n)")
            e.activation(rf, psf[:, 6 * 512:6 * 512 + NT], ACT.Copy).then_inc(x_rms.sem, 1)

        def x_dve(e, ch):
            for k in range(KT):
                e.wait_ge(*x_hi(k + 1))
                s = 2 * (k % 3)
                e.scalar_tensor_tensor(out=h_lo[:, k, :], in0=psf[:, s * 512:s * 512 + NT],
                                       scalar=pcol[:, R_LNMIX + k:R_LNMIX + k + 1],
                                       in1=h_hi[:, k, :].bitcast(F32), op0=ALU.mult,
                                       op1=ALU.subtract).then_inc(x_lo.sem, 1)

        def rstd_dve(e, ch):
            e.wait_ge(*x_sq(1))
            ch.step(e.reciprocal(rstd, rms))
            ch.settle()
            for t in range(4):
                e.tensor_scalar(diag[:, t, :], ident[:], rstd[:, t:t + 1], None, ALU.mult).then_inc(x_diag.sem, 1)
            e.tensor_scalar(diag_s[:], ident[0:NB, 0:NB], rstd[0:NB, 4:5], None, ALU.mult).then_inc(x_diag.sem, 1)

        def x_pe(e):
            e.wait_ge(c_kout, N_ST)
            e.wait_ge(c_vout, N_ST)
            for t in range(5):
                e.wait_ge(xs_ld[t], 16)
            for k in range(KT):
                s = 2 * (k % 3)
                if k >= 3:
                    e.wait_ge(*x_lo(k - 2))
                for t in range(4):
                    e.transpose(PS[:, s, t * P:t * P + P], xtok[:, t, k * P:k * P + P], ident[:])
                e.transpose(PS[:, s + 1, 0:NB], xs_tok[:, k * P:k * P + P],
                            ident[0:NB, 0:NB]).then_inc(x_turned.sem, 1)

        def rstd_pe(e):
            e.wait_ge(*x_diag(5))
            e.matmul(PS[:, 6, :], ones[:], diag[:].rearrange("p t n -> p (t n)"), start=True, stop=True)
            e.matmul(PS[:, 7, 0:NB], ones[0:NB, :], diag_s[:], start=True, stop=True).then_inc(x_bcd.sem, 1)

        w_land = [sem(f"w_land{n}") for n in range(N_RAW)]
        win_out = sem("win_out")
        w_hi_rdy, w_lo_rdy, w_used = sem("w_hi_rdy"), sem("w_lo_rdy"), sem("w_used")
        g_out = sem("g_out")

        def load_piece(e, n, n0, parts, first=False):
            if not first:
                e.wait_ge(w_lo_rdy, n - N_RAW + 1)
            assert len(parts) == 2
            for dst, src in parts:
                e.dma_start(dst, src).then_inc(w_land[n0 % N_RAW], 16)

        def split_views(n0, paired):
            hi, lo, raw = w_hi[:, n0 % N_SPLIT], w_lo[:, n0 % N_SPLIT], w_raw[:, n0 % N_RAW]
            if not paired:
                return [(hi, lo, raw)]
            place = lambda w: w.rearrange("p k (m a d) -> p k m a d", m=2, a=2)
            return [(place(hi)[:, :, :, a, :], place(lo)[:, :, :, a, :],
                     raw[:, :, a * P:a * P + P].rearrange("p k (m d) -> p k m d", m=2)) for a in range(2)]

        def hi_piece(e, n, n0, uses, first=False, paired=False):
            e.wait_ge(w_land[n0 % N_RAW], 32 * uses)
            if not first:
                e.wait_ge(w_used, n - N_SPLIT + 1)
            for hi, _, raw in split_views(n0, paired):
                ins = e.activation(hi, raw, ACT.Copy)
            ins.then_inc(w_hi_rdy, 1)

        def lo_piece(e, n, n0, paired=False):
            e.wait_ge(w_hi_rdy, n + 1)
            for hi, lo, raw in split_views(n0, paired):
                ins = e.tensor_tensor(lo, raw, hi.bitcast(F32), ALU.subtract)
            ins.then_inc(w_lo_rdy, 1)

        def mul_piece(e, n, n0, bank, hi, lo, k0, first, last, tiles=2):
            e.wait_ge(w_lo_rdy, n + 1)
            s = n0 % N_SPLIT
            for k in range(PK):
                for m in range(tiles):
                    st, sp = first and k == 0, last and k == PK - 1
                    wh, wl = w_hi[:, s, k, m * P:m * P + P], w_lo[:, s, k, m * P:m * P + P]
                    for c, (w, x) in enumerate(((wh, hi), (wh, lo), (wl, hi))):
                        for h in range(2):
                            mm = e.matmul(PS[:, bank + 2 * m + h, 0:HN], w, x[:, k0 + k, h * HN:h * HN + HN],
                                          start=st and c == 0, stop=sp and c == 2)
            mm.then_inc(w_used, 1)

        def pair_src(w, k0, col):
            return [w[(k0 + 2 * z) * P:(k0 + 2 * z + 2) * P, col].rearrange("(k p) n -> p k n", p=P)
                    for z in range(2)]

        w_in = i["w_in"][0]

        def proj_sp(e):
            wq = w_in[:, 0:1024].rearrange("(k p) (gp a r n) -> p k gp a r n", p=P, gp=2, a=2, r=2)
            n = 0
            for blk in range(4):
                for kp in range(4):
                    s = n % N_RAW
                    if n % 2:
                        b = n // 2
                        e.dma_start(o["kv_win_s"][0, b, 0:WIN - 1], i["state_kv_win"][0, b, 1:WIN]).then_inc(win_out, 16)
                    load_piece(e, n, n, [
                        (w_raw[:, s, :, a * P:a * P + P],
                         wq[:, kp * PK:kp * PK + PK, blk // 2, a, blk % 2]) for a in range(2)], first=n < N_RAW)
                    n += 1

            def regular(n, blocks, col0):
                with e.Fori(0, blocks // 2) as it:
                    for z in range(8):
                        s = z % N_RAW
                        col = it * (2 * PN) + (col0 + (z // 4) * PN)
                        src = pair_src(w_in, (z % 4) * PK, bass.ds(col, PN))
                        load_piece(e, it * 8 + (n + z), z, [
                            (w_raw[:, s, 2 * y:2 * y + 2, :], src[y]) for y in range(2)])
            regular(16, 6, C_KV)
            regular(16 + 24, 10, C_Z)
            for kp in range(4):
                n = IN_PIECES + kp
                rows_k = slice(kp * PK * P, (kp + 1) * PK * P)
                load_piece(e, n, n, [
                    (w_raw[:, n % N_RAW, :, at_:at_ + w],
                     w_in[rows_k, c:c + w].rearrange("(k p) n -> p k n", p=P))
                    for at_, w, c in ((0, 48, C_GATE), (DT0, NH, C_DT))])

        def proj_act(e, ch):
            for n in range(Q_PIECES + 2):
                hi_piece(e, n, n, n // N_RAW + 1, first=n < N_SPLIT, paired=n < Q_PIECES)
                if n < 4:
                    square_sum(e, ch, n)
                if n == 4:
                    token_rms(e, ch)
            with e.Fori(Q_PIECES // 8, IN_BLOCKS // 2) as it:
                for z in range(2, 10):
                    hi_piece(e, it * 8 + z, z, it * 2 + (z // 4 + 1))
            hi_piece(e, IN_PIECES + 2, 2, IN_PIECES // 4 + 1)
            hi_piece(e, IN_PIECES + 3, 3, IN_PIECES // 4 + 1)

        def proj_out(e, tile, bank):
            e.tensor_tensor(proj[:, tile], PS[:, bank:bank + 2, 0:HN], rstd_bc[:], ALU.mult).then_inc(g_out, 1)

        def proj_dve(e, ch):
            for n in range(Q_PIECES + 2):
                lo_piece(e, n, n, paired=n < Q_PIECES)
                if n == 4:
                    rstd_dve(e, ch)
                    e.wait_ge(*x_rms(1))
                if n >= 5 and n % 4 == 1:
                    for m in range(2):
                        proj_out(e, 2 * (n // 4 - 1) + m, 4 * ((n // 4 - 1) % 2) + 2 * m)
            with e.Fori(Q_PIECES // 8, IN_BLOCKS // 2) as it:
                for z in range(2, 10):
                    lo_piece(e, it * 8 + z, z)
                    if z in (5, 9):
                        for m in range(2):
                            proj_out(e, it * 4 + (2 * (z // 8) + m), 4 * (z // 8) + 2 * m)
            lo_piece(e, IN_PIECES + 2, 2)
            lo_piece(e, IN_PIECES + 3, 3)
            e.wait_ge(w_used, IN_PIECES + GD_PIECES)
            proj_out(e, T_GD, 0)

        def proj_pe(e):
            def block(n, n0, bank):
                for kp in range(4):
                    e.wait_ge(*x_lo(PK * (kp + 1)))
                    mul_piece(e, n + kp, n0 + kp, bank, h_hi, h_lo, kp * PK, kp == 0, kp == 3)
            block(0, 0, 0)
            rstd_pe(e)
            e.wait_ge(*x_rms(1))
            block(4, 4, 4)
            with e.Fori(1, IN_BLOCKS // 2) as it:
                for half in range(2):
                    e.wait_ge(g_out, it * 4 + (2 * half - 2))
                    block(it * 8 + 4 * half, 4 * half, 4 * half)
            e.wait_ge(g_out, 2 * IN_BLOCKS - 2)
            for kp in range(GD_PIECES):
                n = IN_PIECES + kp
                mul_piece(e, n, n, 0, h_hi, h_lo, kp * PK, kp == 0, kp == 3, tiles=1)

        kv_tok = at("kv_tok", [P, 4, 3 * KVW], A1)
        kvs_tok = at("kvs_tok", [NB, 3 * KVW], A1 + 24576)
        xl_tok = at("xl_tok", [3 + NB, CONV_DIM], M_HI)
        cmp_rows_out = sem("cmp_rows_out")
        r_turned, r_act, r_dve, q_scaled, rows_out = (
            sem(n) for n in ("r_turned", "r_act", "r_dve", "q_scaled", "rows_out"))
        R_FILLS = []
        for c in range(3):
            for t in range(4):
                R_FILLS.append((kv_tok[:, t, c * KVW:(c + 1) * KVW], P,
                                [pt[:, T_KC + 4 * c + x, t * P:t * P + P] for x in range(4)]))
        for c in range(3):
            R_FILLS.append((kvs_tok[:, c * KVW:(c + 1) * KVW], NB,
                            [pt[:, T_KC + 4 * c + x, SEQ:NT] for x in range(4)]))
        for c in range(3):
            R_FILLS.append((xl_tok[:, c * 512:(c + 1) * 512], 3 + NB,
                            [pt[:, T_X + 4 * c + x, SEQ - 3:NT] for x in range(4)]))

        def rows_pe(e):
            e.wait_ge(g_out, NTILE)
            for f, (_, n, srcs) in enumerate(R_FILLS):
                if f >= 8:
                    e.wait_ge((r_act, r_dve)[f % 2], f // 2 - 3)
                for x, src in enumerate(srcs):
                    last = e.transpose(PS[0:n, f % 8, x * P:x * P + P], src, ident[:])
                last.then_inc(r_turned, 1)

        def rows_copy(e, par, copy, done):
            for f, (dst, n, _) in enumerate(R_FILLS):
                if f % 2 == par:
                    e.wait_ge(r_turned, f + 1)
                    copy(dst, PS[0:n, f % 8, :]).then_inc(done, 1)

        def rows_act(e):
            rows_copy(e, 0, lambda a, b: e.activation(a, b, ACT.Copy), r_act)

        def rows_dve(e):
            rows_copy(e, 1, lambda a, b: e.tensor_copy(a, b), r_dve)
            e.wait_ge(g_out, NTILE)
            e.tensor_scalar(pt[:, T_Q:T_Q + 8, :], pt[:, T_Q:T_Q + 8, :], HD ** -0.5, None,
                            ALU.mult).then_inc(q_scaled, 1)

        def rows_sp(e):
            for c, name in enumerate(("kv_cmp_p", "kv_sel_p", "kv_win_p")):
                if c < 2:
                    e.wait_ge(r_act, (2, len(R_FILLS) // 2)[c])
                    e.wait_ge(r_dve, (2, len(R_FILLS) // 2)[c])
                e.dma_start(o[name].rearrange("a b (t p) c g d -> p (a b t) (c g d)", p=P),
                            kv_tok[:, :, c * KVW:(c + 1) * KVW]).then_inc(rows_out if c else cmp_rows_out, 16)
                if c == 0:
                    cmp_p_load(e)
            for c, name in enumerate(("kv_cmp_s", "kv_sel_s")):
                e.dma_start(o[name].rearrange("a b t c g d -> (a b t) (c g d)"),
                            kvs_tok[:, c * KVW:(c + 1) * KVW]).then_inc(rows_out, 16)
            e.dma_start(o["kv_win_s"][0, :, WIN - 1].rearrange("b c g d -> b (c g d)"),
                        kvs_tok[:, 2 * KVW:3 * KVW]).then_inc(rows_out, 16)
            e.dma_start(o["conv_p"][0, 0], xl_tok[0:3, :]).then_inc(rows_out, 16)
            e.dma_start(o["conv_s"][0, :, 2], xl_tok[3:3 + NB, :]).then_inc(rows_out, 16)
            e.dma_start(o["conv_s"][0, :, 0:2], i["state_conv"][0, :, 1:3]).then_inc(rows_out, 16)
        N_ROWS_OUT = 8

        segp = at("segp", [32, STRIDE, 8, HD], A0)
        segp_ord = at("segp_ord", [32, 8, STRIDE, HD], M_RING)
        w1p = at("w1p", [P, 2, 16, CHID], A0)
        segp_T = at("segp_T", [P, 8, 8, 32], A2 + T_KC * TILE)
        second_p = at("second_p", [P, 2, NKV, 32], A1 + 30720)
        hid_p = at("hid_p", [P, 2, NKV, 32], A1 + 31744)
        hidp_s = at("hidp_s", [P, 2, NKV, 32], MF + 9216)
        p_ld = sem("p_ld")
        w1p_ld, v_bd, v_zero = sem("w1p_ld"), sem("v_bd"), sem("v_zero")

        def cmp_p_load(e):
            e.wait_ge(cmp_rows_out, 16)
            e.dma_start(segp[:].rearrange("s j c d -> s (j c d)"),
                        o["kv_cmp_p"].rearrange("a b (s j) c g d -> (a b s) (j c g d)", j=STRIDE)).then_inc(p_ld, 16)

        def cmp_p_sp(e):
            e.wait_ge(*p_order(1))
            e.dma_start(w1p[:], i["cmp_w1"].rearrange("a c (l j) d f -> (a j d) c l f", j=2)).then_inc(w1p_ld, 16)

        def values_sp(e):
            e.wait_ge(*p_out(3))
            e.wait_ge(v_zero, 1)
            for t in range(4):
                e.dma_start(vbd[32 * t:32 * t + NCMP_P, :, t, :],
                            vcp[0:NCMP_P, :].rearrange("p (g d) -> p g d", d=HD)).then_inc(v_bd, 16)

        def values_pool(e):
            e.wait_ge(*p_order(1))
            e.memset(vbd[:], 0.0).then_inc(v_zero, 1)

        def cmp_p_pe(e):
            e.wait_ge(*p_order(1))
            for cg in range(8):
                if cg >= 4:
                    e.wait_ge(*p_ev(cg - 3))
                for j in range(8):
                    last = e.transpose(PS[:, cg % 4, j * 32:j * 32 + 32],
                                       segp_ord[:, cg, 2 * j:2 * j + 2, :].rearrange("p j d -> p (j d)"),
                                       ident[0:32, 0:32])
                last.then_inc(p_turned.sem, 1)
            e.wait_ge(*p_ev(8))
            e.wait_ge(w1p_ld, 16)
            for r in (1, 0):
                for c in range(2):
                    for j in range(8):
                        last = e.matmul(PS[:, 4 + 2 * c + r, 0:P], w1p[:, c, r * 8 + j, :],
                                        segp_T[:, 4 * c:4 * c + 4, j, :], start=(j == 0), stop=(j == 7))
                    last.then_inc(p_prod.sem, 1)
            e.wait_ge(*p_silu(1))
            for g in range(NKV):
                last = e.matmul(PS[(g % 2) * HD:(g % 2) * HD + HD, 0, (g // 2) * 32:(g // 2) * 32 + NCMP_P],
                                w2[:, 0, :], hidp_s[:, 0, g, 0:NCMP_P], start=True, stop=True)
            last.then_inc(p_w2.sem, 1)
            e.wait_ge(*p_silu(2))
            for g in range(NKV):
                last = e.matmul(PS[0:NCMP_P, 1, g * HD:g * HD + HD], hidp_s[:, 1, g, 0:NCMP_P], w2[:, 1, :],
                                start=True, stop=True)
            last.then_inc(p_w2.sem, 1)

        def cmp_p_act(e):
            for c in range(2):
                e.wait_ge(*p_prod(c + 1))
                e.activation(second_p[:, c].rearrange("p g n -> p (g n)"), PS[:, 5 + 2 * c, 0:P],
                             ACT.Copy).then_inc(p_half.sem, 1)
            for c in range(2):
                e.wait_ge(*p_sum(c + 1))
                e.activation(hidp_s[:, c, :, 0:NCMP_P], hid_p[:, c, :, 0:NCMP_P], ACT.Silu,
                             bias=bias1[:, c:c + 1]).then_inc(p_silu.sem, 1)

        def cmp_p_dve(e):
            e.wait_ge(p_ld, 16)
            e.wait_ge(rows_out, 16 * N_ROWS_OUT)
            e.tensor_copy(segp_ord[:].rearrange("p c j d -> p j c d"), segp[:]).then_inc(p_order.sem, 1)
            for cg in range(8):
                e.wait_ge(*p_turned(cg + 1))
                e.tensor_copy(segp_T[:, cg], PS[:, cg % 4, 0:256].rearrange("p (j s) -> p j s", j=8)).then_inc(p_ev.sem, 1)
            for c in range(2):
                e.wait_ge(*p_prod(3 + c))
                e.wait_ge(*p_half(1 + c))
                e.tensor_tensor(hid_p[:, c, :, 0:NCMP_P],
                                PS[:, 4 + 2 * c, 0:P].rearrange("p (g n) -> p g n", n=32)[:, :, 0:NCMP_P],
                                second_p[:, c, :, 1:32], ALU.add).then_inc(p_sum.sem, 1)
            e.wait_ge(*p_w2(1))
            for gp in range(2):
                e.tensor_scalar(kcp_T[:, gp, 0:NCMP_P], PS[:, 0, gp * 32:gp * 32 + NCMP_P],
                                pcol[:, R_B2K:R_B2K + 1], None, ALU.add).then_inc(p_out.sem, 1)
            e.wait_ge(*p_w2(2))
            e.tensor_tensor(vcp[0:NCMP_P, :].rearrange("p (g d) -> p g d", d=HD),
                            PS[0:NCMP_P, 1, 0:256].rearrange("p (g d) -> p g d", d=HD),
                            b2v_bc[0:NCMP_P, :].unsqueeze(1).to_broadcast([NCMP_P, NKV, HD]),
                            ALU.add).then_inc(p_out.sem, 1)

        mixf = at("mixf", [P, KT, NT], A0)
        att = at("att", [P, 4, NH * HD], M_RING)
        gates = at("gates", [P, 4, 48], M_RING + 16384)
        gates_s = at("gates_s", [NB, 48], M_RING + 16384 + 768)
        AB = M_RING + 17408
        cm_r = at("cm_r", [P, P], AB, F32R)
        id_r = at("id_r", [P, P], AB + 512, F32R)
        prob = at("prob", [P, 2, 2, SEQ], A0)
        probT = at("probT", [P, 2, 2, SEQ], A0 + 8192)
        o_sc = at("o_sc", [P, 2, 8, HD], A0 + 16384)
        pc = [at(f"pc{x}", [P, 16, 32], (A0 + 20480, A0)[x]) for x in range(2)]
        pc_e = [at(f"pc_e{x}", [P, 16, 32], (A0 + 22528, A0 + 2048)[x]) for x in range(2)]
        pcT = at("pcT", [P, 4, P], A0 + 24576)
        vbd = at("vbd", [P, NKV, 4, HD], A0 + 26624)
        negmax = at("negmax", [P, 2, 8], AB + 1024)
        den = at("den", [P, 2, 8], AB + 1088)
        fac = at("fac", [P, 2, 8], AB + 1152)
        rec = at("rec", [P, 2, 8], AB + 1216)
        cmx, cden, crec, cfac = (at(n, [P, 2, 16], AB + 1280 + 128 * z) for z, n in enumerate(("cmx", "cden", "crec", "cfac")))

        a_gT = sem("a_gT")
        ac_s, ac_sub, ac_exp, ac_p, ac_T, ac_Tc, ac_o, ac_done = (
            sem(n) for n in ("ac_s", "ac_sub", "ac_exp", "ac_p", "ac_T", "ac_Tc", "ac_o", "ac_done"))
        as_s, as_max, as_exp, as_T, as_Tsel, as_Twin, as_pv, as_out = (
            sem(n) for n in ("as_s", "as_max", "as_exp", "as_T", "as_Tsel", "as_Twin", "as_pv", "as_out"))

        def q_of(head, qt):
            g, r = head // 4, head % 4
            a = g % 2
            return pt[a * HD:a * HD + HD, T_Q + (g // 2) * 4 + r, qt * P:qt * P + P]

        def k_of(tile0, g, keys):
            a = g % 2
            return pt[a * HD:a * HD + HD, tile0 + g // 2, keys]

        def gate_pe(e):
            e.wait_ge(r_act, len(R_FILLS) // 2)
            e.wait_ge(r_dve, len(R_FILLS) // 2)
            e.wait_ge(*p_out(3))
            for qt in range(4):
                e.transpose(PS[:, 0, qt * 48:qt * 48 + 48], pt[0:48, T_GD, qt * P:qt * P + P], ident[0:48, 0:48])
            e.transpose(PS[0:NB, 0, 192:240], pt[0:48, T_GD, SEQ:NT], ident[0:48, 0:48]).then_inc(a_gT, 1)

        def gate_act(e):
            e.wait_ge(a_gT, 1)
            e.activation(gates[:], PS[:, 0, 0:192].rearrange("p (t n) -> p t n", n=48), ACT.Sigmoid).then_inc(a_gate.sem, 1)
            e.activation(gates_s[:], PS[0:NB, 0, 192:240], ACT.Sigmoid).then_inc(a_gate.sem, 1)
            e.activation(cm_r[:], cmask[:], ACT.Copy).then_inc(a_mask.sem, 1)
            e.activation(id_r[:], ident[:], ACT.Copy).then_inc(a_mask.sem, 1)

        def att_cmp_pe(e):
            e.wait_ge(*a_gate(2))
            e.wait_ge(q_scaled, 1)

            def scores(g):
                a = g % 2
                if g >= 2:
                    e.wait_ge(ac_sub, g - 1)
                for r in range(4):
                    for qt in range(4):
                        last = e.matmul(PS[:, 7 * a, (r * 4 + qt) * 32:(r * 4 + qt) * 32 + 32], q_of(4 * g + r, qt),
                                        kcp_T[a * HD:a * HD + HD, g // 2, :], start=True, stop=True)
                last.then_inc(ac_s, 1)

            scores(0)
            for g in range(NKV):
                if g + 1 < NKV:
                    scores(g + 1)
                e.wait_ge(ac_p, g + 1)
                for r in range(4):
                    last = e.transpose(PS[:, 1, r * P:r * P + P],
                                       pc_e[g % 2][:, 4 * r:4 * r + 4, :].rearrange("p t n -> p (t n)"), ident[:])
                last.then_inc(ac_T, 1)
                e.wait_ge(ac_Tc, g + 1)
                if g:
                    e.wait_ge(ac_done, g)
                if g == 0:
                    e.wait_ge(v_bd, 16 * 4)
                for r in range(4):
                    last = e.matmul(PS[:, 5 + r // 2, (r % 2) * 256:(r % 2) * 256 + 256], pcT[:, r, :],
                                    vbd[:, g].rearrange("p t d -> p (t d)"), start=True, stop=True)
                last.then_inc(ac_o, 1)

        def att_cmp_dve(e, ch):
            gv = gates[:].rearrange("p t (h b) -> p h t b", b=3)

            def shifted(g):
                p, mx = pc[g % 2], cmx[:, g % 2]
                e.wait_ge(ac_s, g + 1)
                ch.step(e.tensor_tensor(p[:].rearrange("p (r t) n -> p r (t n)", r=4),
                                        PS[:, 7 * (g % 2), :].rearrange("p (r x) -> p r x", r=4),
                                        cmpmask[:].rearrange("p t n -> p (t n)").unsqueeze(1)
                                        .to_broadcast([P, 4, P]), ALU.add))
                ch.settle()
                ch.step(e.tensor_reduce(mx, p[:], AX.X, ALU.max))
                ch.settle()
                e.tensor_tensor(p[:], p[:], mx.unsqueeze(2).to_broadcast([P, 16, 32]), ALU.subtract).then_inc(ac_sub, 1)

            def normed(g):
                p, dn, rc, fc = pc_e[g % 2], cden[:, g % 2], crec[:, g % 2], cfac[:, g % 2]
                e.wait_ge(ac_exp, g + 1)
                ch.step(e.tensor_reduce(dn, p[:], AX.X, ALU.add))
                ch.settle()
                ch.step(e.reciprocal(rc, dn))
                ch.settle()
                ch.step(e.tensor_tensor(fc.rearrange("p (r t) -> p r t", t=4), rc.rearrange("p (r t) -> p r t", t=4),
                                        gv[:, 4 * g:4 * g + 4, :, 0], ALU.mult))
                ch.settle()
                ch.step(e.tensor_scalar(cfac[:, g % 2, 0:16:4], cfac[:, g % 2, 0:16:4], valid0[:, 0:1], None, ALU.mult))
                ch.settle()
                e.tensor_tensor(p[:], p[:], fc.unsqueeze(2).to_broadcast([P, 16, 32]), ALU.mult).then_inc(ac_p, 1)

            shifted(0)
            for g in range(NKV):
                if g + 1 < NKV:
                    shifted(g + 1)
                normed(g)
                if g:
                    outputs(e, g - 1)
            outputs(e, NKV - 1)

        def outputs(e, g):
            e.wait_ge(ac_o, g + 1)
            for half in range(2):
                dst = att[:, :, (4 * g + 2 * half) * HD:(4 * g + 2 * half + 2) * HD]
                last = e.tensor_copy(dst.rearrange("p t (r d) -> p r t d", r=2),
                                     PS[:, 5 + half, :].rearrange("p (r t d) -> p r t d", r=2, t=4))
            last.then_inc(ac_done, 1)

        def att_cmp_act(e):
            for g in range(NKV + 1):
                if g < NKV:
                    e.wait_ge(ac_sub, g + 1)
                    if g >= 2:
                        e.wait_ge(ac_T, g - 1)
                    e.activation(pc_e[g % 2][:], pc[g % 2][:], ACT.Exp).then_inc(ac_exp, 1)
                if g:
                    e.wait_ge(ac_T, g)
                    if g >= 2:
                        e.wait_ge(ac_o, g - 1)
                    e.activation(pcT[:], PS[:, 1, :].rearrange("p (r n) -> p r n", n=P), ACT.Copy)\
                     .then_inc(ac_Tc, 1)

        NU = NH * 4
        BR = ((T_KS, KVW), (T_KW, 2 * KVW))

        def att_pe(e):
            e.wait_ge(*a_mask(2))
            e.wait_ge(ac_done, NKV)

            def scores(u):
                h, qt = divmod(u, 4)
                if u >= 2:
                    e.wait_ge(as_exp, 2 * (u - 1))
                w = (qt + 1) * P
                for b, (kt, _) in enumerate(BR):
                    bank = 2 * (u % 2) + b
                    e.matmul(PS[:, bank, 0:w], q_of(h, qt), k_of(kt, h // 4, slice(0, w)), start=True, stop=False)
                    last = e.matmul(PS[:, bank, qt * P:w], id_r[:], cm_r[:], start=False, stop=True)
                last.then_inc(as_s, 1)

            def turn(u):
                qt = u % 4
                e.wait_ge(as_exp, 2 * (u + 1))
                if u:
                    e.wait_ge(as_Tsel, u)
                    e.wait_ge(as_Twin, u)
                for b in range(2):
                    for k in range(qt + 1):
                        last = e.transpose(PS[:, 4 + b, k * P:k * P + P], prob[:, u % 2, b, k * P:k * P + P], ident[:])
                last.then_inc(as_T, 1)

            def values(u):
                h, qt = divmod(u, 4)
                e.wait_ge(as_Tsel, u + 1)
                e.wait_ge(as_Twin, u + 1)
                if qt == 0 and h >= 2:
                    e.wait_ge(as_out, h - 1)
                for b, (_, col) in enumerate(BR):
                    c = col + KVW // 2 + (h // 4) * HD
                    for k in range(qt + 1):
                        last = e.matmul(PS[:, 6 + h % 2, (2 * qt + b) * HD:(2 * qt + b) * HD + HD],
                                        probT[:, u % 2, b, k * P:k * P + P], kv_tok[:, k, c:c + HD],
                                        start=(k == 0), stop=(k == qt))
                last.then_inc(as_pv, 1)

            scores(0)
            for u in range(NU):
                if u + 1 < NU:
                    scores(u + 1)
                if u:
                    values(u - 1)
                turn(u)
            values(NU - 1)

        def att_act(e):
            for u in range(NU):
                qt = u % 4
                w = (qt + 1) * P
                h = u // 4
                if u >= 2:
                    e.wait_ge(as_T, u - 1)
                if qt == 0 and h >= 2:
                    e.wait_ge(as_out, h - 1)
                for b in range(2):
                    e.wait_ge(as_max, 2 * u + b + 1)
                    e.activation(prob[:, u % 2, b, 0:w], PS[:, 2 * (u % 2) + b, 0:w], ACT.Exp,
                                 bias=negmax[:, h % 2, 2 * qt + b:2 * qt + b + 1],
                                 accum_out=den[:, h % 2, 2 * qt + b:2 * qt + b + 1]).then_inc(as_exp, 1)
                if u:
                    window_turned(e, u - 1)
            window_turned(e, NU - 1)

        def window_turned(e, u):
            w = (u % 4 + 1) * P
            e.wait_ge(as_T, u + 1)
            if u >= 2:
                e.wait_ge(as_pv, u - 1)
            e.activation(probT[:, u % 2, 1, 0:w], PS[:, 5, 0:w], ACT.Copy).then_inc(as_Twin, 1)

        def att_dve(e, ch):
            gv = gates[:].rearrange("p t (h b) -> p h t b", b=3)

            def row_max(u):
                h, qt = divmod(u, 4)
                e.wait_ge(as_s, u + 1)
                if qt == 0 and h >= 2:
                    e.wait_ge(as_exp, 8 * (h - 1))
                for b in range(2):
                    e.tensor_reduce(negmax[:, h % 2, 2 * qt + b:2 * qt + b + 1],
                                    PS[:, 2 * (u % 2) + b, 0:(qt + 1) * P], AX.X, ALU.max,
                                    negate=True).then_inc(as_max, 1)

            def head_out(h):
                e.wait_ge(as_exp, 8 * (h + 1))
                ch.step(e.reciprocal(rec[:, h % 2], den[:, h % 2]))
                ch.settle()
                ch.step(e.tensor_tensor(fac[:, h % 2].rearrange("p (t b) -> p t b", b=2),
                                        rec[:, h % 2].rearrange("p (t b) -> p t b", b=2),
                                        gv[:, h, :, 1:3], ALU.mult))
                ch.settle()
                if h >= 2:
                    e.wait_ge(att_add, 2 * (h - 1))
                e.wait_ge(as_pv, 4 * (h + 1))
                e.tensor_tensor(o_sc[:, h % 2], PS[:, 6 + h % 2, :].rearrange("p (x d) -> p x d", d=HD),
                                fac[:, h % 2].unsqueeze(2).to_broadcast([P, 8, HD]), ALU.mult).then_inc(as_out, 1)

            e.wait_ge(ac_done, NKV)
            row_max(0)
            for u in range(NU):
                if u + 1 < NU:
                    row_max(u + 1)
                w = (u % 4 + 1) * P
                e.wait_ge(as_T, u + 1)
                if u >= 2:
                    e.wait_ge(as_pv, u - 1)
                e.tensor_copy(probT[:, u % 2, 0, 0:w], PS[:, 4, 0:w]).then_inc(as_Tsel, 1)
                if u % 4 == 1 and u >= 4:
                    head_out(u // 4 - 1)
            head_out(NH - 1)

        def att_pool(e):
            e.wait_ge(ac_done, NKV)
            for h in range(NH):
                e.wait_ge(as_out, h + 1)
                dst = att[:, :, h * HD:h * HD + HD]
                for b in range(2):
                    if b:
                        e.wait_ge(att_add, 2 * h + 1)
                    src = o_sc[:, h % 2].rearrange("p (t b) d -> p t b d", b=2)[:, :, b, :]
                    e.tensor_tensor(dst, dst, src, ALU.add).then_inc(att_rdy if (h, b) == (NH - 1, 1) else att_add, 1)

        att_add = sem("att_add")

        att_rdy, m_turned, m_out = sem("att_rdy"), sem("m_turned"), sem("m_out")

        MIX_BANK = (0, 1, 4, 6)

        def att_mix_pe(e):
            e.wait_ge(att_rdy, 1)
            for t in range(8):
                if t >= 4:
                    e.wait_ge(m_out, t - 3)
                for qt in range(4):
                    last = e.transpose(PS[:, MIX_BANK[t % 4], qt * P:qt * P + P], att[:, qt, t * P:t * P + P], ident[:])
                last.then_inc(m_turned, 1)

        def att_mix_act(e):
            for t in range(8):
                e.wait_ge(m_turned, t + 1)
                e.activation(mixf[:, t, 0:SEQ], PS[:, MIX_BANK[t % 4], :], ACT.Copy).then_inc(m_out, 1)

        PV_ORDER = (6, 7, 0, 1, 2, 3, 4, 5)
        NS = 4
        sel_t = at("sel_t", [P, 2, 8, KVW], M_RING)
        sel_x = at("sel_x", [P, 8, KVW], A2)
        SEL = (sel_t[:, 0], sel_t[:, 1], sel_x[:])
        o_t = at("o_t", [NH, NB, 256], A2 + 16384)
        win_t = at("win_t", [P, NS, 4, 256], A1)
        qz = at("qz", [P, 2, NB, P], A2 + T_KC * TILE)
        kT_s = at("kT_s", [P, 2, 2, 1024], A2)
        kT_w = at("kT_w", [P, 2, 2, SEQ], A1 + 16384)
        pr_s = at("pr_s", [P, 1032], A2 + 24576)
        pr_w = at("pr_w", [P, SEQ], A2 + 28736)
        pT_s = at("pT_s", [P, 8, P], A2 + 30784)
        pT_w = at("pT_w", [P, 4, P], A2 + 34880)
        diag_n = at("diag_n", [P, P], A2 + 36928)
        o_s = at("o_s", [P, P], A2 + 37440)
        swapm = at("swapm", [P, P], A2 + 37952)
        pnz = at("pnz", [NB, P], A2 + 38464)
        pn = at("pn", [P, 64], MF + 9216)
        pg = at("pg", [P, 64], MF + 9472)
        pnT = at("pnT", [64, P], MF + 9728)
        pgT = at("pgT", [64, P], MF + 10240)
        ksn = at("ksn", [P, 2, NB], MF + 10752)
        imp1 = at("imp1", [P, 17], MF + 10816)
        imp = at("imp", [P, 17], MF + 10912)
        eqb = at("eqb", [P, 17], MF + 11008)
        dropadd = at("dropadd", [P, 17], MF + 11104)
        gbh = at("gbh", [P, 3], MF + 11200)
        sden = at("sden", [P, 4], MF + 11232)
        smax = at("smax", [P, 4], MF + 11264)
        srec = at("srec", [P, 4], MF + 11296)
        sfac = at("sfac", [P, 4], MF + 11328)
        smn = at("smn", [P, 2], MF + 11360)

        n_ld = [sem(f"n_ld{x}") for x in range(3)]
        nw_ld = [sem(f"nw_ld{x}") for x in range(NS)]
        n_free, nc_exp = (
            sem(n) for n in ("n_free", "nc_exp"))
        n_fill, n_ev_a, n_ev_d, n_sc, n_exp, n_pT, n_pTc, n_v, n_oT, n_sw, n_gate = (
            sem(n) for n in ("n_fill", "n_ev_a", "n_ev_d", "n_sc", "n_exp", "n_pT", "n_pTc", "n_v", "n_oT", "n_sw", "n_gate"))
        def win_parts():
            return ((0, 112, 4), (112, 127, 4), (127, 128, 3))

        def smp_sp(e):
            e.wait_ge(*a_gate(2))
            e.dma_start(gbh[:], gates_s[:].rearrange("b (h n) -> b h n", n=3)).then_inc(n_gate, 16)
            e.wait_ge(att_rdy, 1)
            e.dma_start(cst[:], i["state_conv"].rearrange("a b w c -> (a b w) c")).then_inc(d_cld, 16)
            for x in range(2 * NB):
                s, half = x % NS, x // NB
                b = PV_ORDER[x - NB] if half else x
                if x >= NS and x - NS < NB:
                    e.wait_ge(n_fill, 6 * (x - NS + 1))
                elif x >= NS:
                    e.wait_ge(n_v, x - NS - NB + 1)
                for p0, p1, nr in win_parts():
                    e.dma_start(win_t[p0:p1, s, 0:nr, :],
                                i["state_kv_win"][0, b, 1 + 4 * p0:1 + 4 * p0 + (p1 - p0 - 1) * 4 + nr, half]
                                .rearrange("(p r) g d -> p r (g d)", r=nr)).then_inc(nw_ld[s], 16)
                e.dma_start(win_t[127:128, s, 3, :],
                            kvs_tok[b:b + 1, 2 * KVW + half * 256:2 * KVW + half * 256 + 256]).then_inc(nw_ld[s], 16)

        def q_pool(e):
            e.wait_ge(*p_prod(4))
            e.memset(qz[:], 0.0).then_inc(n_free, 1)

        def smp_pool(e, ch):
            e.wait_ge(m_turned, 8)
            e.wait_ge(n_gate, 16)
            rows_s = i["cache_kv_sel"].rearrange("a n (s j) c g d -> (a n s) (j c g d)", j=8)
            def gather(b, slot):
                e.indirect_dma_start(
                    out=SEL[slot].rearrange("p j c -> p (j c)"), out_offset=None, in_=rows_s,
                    in_offset=bass.IndirectOffsetOnAxis(ap=idx_s[:, b:b + 1], axis=0)).then_inc(n_ld[slot], 16)

            for b in range(NB):
                if b >= 2:
                    e.wait_ge(n_fill, 6 * (b - 1))
                gather(b, b % 2)
            for x in range(2, NB):
                if x == 2:
                    e.wait_ge(n_sc, NB)
                else:
                    e.wait_ge(n_v, x - 2)
                gather(PV_ORDER[x], x % 3)

        def smp_cmp_pe(e):
            e.wait_ge(as_exp, 2 * NU)
            e.wait_ge(*n_q(1))
            for b in range(NB):
                for gp in range(2):
                    e.matmul(PS[:, 3, 0:NCMP_S], qz[:, gp, b, :], kc_T[:, gp, b, 0:NCMP_S],
                             start=(b + gp == 0), stop=(b + gp == NB))
            for b in range(NB):
                for gp in range(2):
                    last = e.matmul(PS[:, 2, 0:1], qz[:, gp, b, :], ksn[:, gp, b:b + 1],
                                    start=(b + gp == 0), stop=(b + gp == NB))
            last.then_inc(nc_s.sem, 1)

        def smp_pe(e):
            e.wait_ge(m_out, 8)
            e.wait_ge(*nc_p(2))
            e.transpose(PS[0:NCMP_S, 5, 0:P], pn[:, 0:NCMP_S], ident[:])
            e.transpose(PS[0:NCMP_S, 5, P:2 * P], pg[:, 0:NCMP_S], ident[:]).then_inc(nc_T.sem, 1)
            e.wait_ge(*nc_Tc(2))
            e.matmul(PS[:, 7, 0:17], pnT[0:NCMP_S, :], sel_mat[0:NCMP_S, :], start=True, stop=True).then_inc(n_imp.sem, 1)
            e.wait_ge(*n_imp1(1))
            e.matmul(PS[:, 7, 32:49], same_grp[:], imp1[:], start=True, stop=True).then_inc(n_imp.sem, 1)
            e.wait_ge(*n_drop(1))

            e.wait_ge(d_cld, 16)
            for k in range(12):
                last = e.transpose(PS[:, 2, P + 24 * k:P + 24 * k + 24], cst[:, k * P:k * P + P], ident[0:24, 0:24])
            last.then_inc(d_ct.sem, 1)

            def fill(b):
                s, sw = b % 2, b % NS
                e.wait_ge(n_ld[s], 16 * (b // 2 + 1))
                e.wait_ge(nw_ld[sw], 64 * (b // NS + 1))
                for x in range(6):
                    f = 6 * b + x
                    if f >= 3:
                        e.wait_ge((n_ev_a, n_ev_d)[(f - 3) % 2], (f - 3) // 2 + 1)
                    for y in range(4):
                        if x < 4:
                            src = sel_t[:, s, 4 * (x % 2) + y, (x // 2) * P:(x // 2) * P + P]
                        else:
                            src = win_t[:, sw, y, (x - 4) * P:(x - 4) * P + P]
                        last = e.transpose(PS[:, 5 + f % 3, y * P:y * P + P], src, ident[:])
                    last.then_inc(n_fill, 1)

            def scores(b):
                e.wait_ge(n_ev_a, 3 * (b + 1))
                e.wait_ge(n_ev_d, 3 * (b + 1))
                s = b % 2
                for gp in range(2):
                    st, sp = b + gp == 0, b + gp == NB
                    for h in range(2):
                        e.matmul(PS[:, h, :], qz[:, gp, b, :], kT_s[:, s, gp, h * 512:h * 512 + 512], start=st, stop=sp)
                    last = e.matmul(PS[:, 4, :], qz[:, gp, b, :], kT_w[:, s, gp, :], start=st, stop=sp)
                last.then_inc(n_sc, 1)

            fill(0)
            for b in range(NB):
                if b + 1 < NB:
                    fill(b + 1)
                scores(b)
            e.wait_ge(n_ev_a, 3 * NB)
            e.wait_ge(n_ev_d, 3 * NB)
            e.wait_ge(*n_pd(3))
            for y in range(8):
                e.transpose(PS[:, 5 + y // 4, (y % 4) * P:(y % 4) * P + P], pr_s[:, y * P:y * P + P], ident[:])
            for y in range(4):
                e.transpose(PS[:, 7, y * P:y * P + P], pr_w[:, y * P:y * P + P], ident[:])
            e.matmul(PS[0:NB, 3, 0:P], own_batch[:], diag_n[:], start=True, stop=True).then_inc(n_pT, 1)
            e.wait_ge(n_pTc, 3)
            for x, b in enumerate(PV_ORDER):
                sw = x % NS
                e.wait_ge(n_ld[x % 3], 16 * (x // 3 + (1 if x % 3 == 2 else NB // 2)))
                e.wait_ge(nw_ld[sw], 64 * ((NB + x) // NS + 1))
                rows_b = slice(b * NH, b * NH + NH)
                out = PS[0:NH, b // 2, (b % 2) * 256:(b % 2) * 256 + 256]
                for y in range(8):
                    e.matmul(out, pT_s[:, y, rows_b], SEL[x % 3][:, y, 256:512], start=(y == 0), stop=False)
                e.matmul(out, pnz[:, rows_b], kvs_tok[:, KVW + 256:2 * KVW], start=False, stop=False)
                e.matmul(out, pgT[0:NCMP_S, rows_b], vc[0:NCMP_S, b, :], start=False, stop=False)
                for y in range(4):
                    last = e.matmul(out, pT_w[:, y, rows_b], win_t[:, sw, y, :], start=False, stop=(y == 3))
                last.then_inc(n_v, 1)
            e.wait_ge(*n_oc(4))
            for gp in range(2):
                for b in range(NB):
                    last = e.transpose(PS[:, 4 + gp, b * NH:b * NH + NH], o_t[:, b, gp * P:gp * P + P], ident[0:NH, 0:NH])
            last.then_inc(n_oT, 1)
            e.wait_ge(*n_o(2))
            e.matmul(PS[:, 1, 0:P], swapm[:], o_s[:], start=True, stop=True).then_inc(n_sw, 1)

        def smp_copy(e, par, copy, done, between):
            for b in range(NB):
                if b >= 2:
                    e.wait_ge(n_sc, b - 1)
                for x in range(par, 6, 2):
                    f = 6 * b + x
                    e.wait_ge(n_fill, f + 1)
                    dst = (kT_s[:, b % 2, x // 2, (x % 2) * 512:(x % 2) * 512 + 512] if x < 4
                           else kT_w[:, b % 2, x - 4, :])
                    copy(dst, PS[:, 5 + f % 3, :]).then_inc(done, 1)
                between(b)

        def smp_cmp_act(e):
            e.wait_ge(*nc_max(1))
            e.activation(pn[:, 0:NCMP_S], PS[:, 3, 0:NCMP_S], ACT.Exp, bias=smax[:, 0:1],
                         accum_out=sden[:, 0:1]).then_inc(nc_exp, 1)

        def smp_act(e):
            smp_copy(e, 0, lambda a, b: e.activation(a, b, ACT.Copy), n_ev_a,
                     lambda b: ssd_prep_act(e, b))
            e.wait_ge(*n_max(1))
            e.activation(pr_w[:], PS[:, 4, :], ACT.Exp, bias=smax[:, 2:3], accum_out=sden[:, 2:3]).then_inc(n_exp, 1)
            e.wait_ge(*n_max(2))
            e.activation(pr_s[:, 0:1025], pr_s[:, 0:1025], ACT.Exp, bias=smax[:, 1:2],
                         accum_out=sden[:, 1:2]).then_inc(n_exp, 1)
            e.wait_ge(n_pT, 1)
            e.activation(pT_s[:].rearrange("p y n -> p (y n)"), psf[:, 5 * 512:7 * 512], ACT.Copy).then_inc(n_pTc, 1)

        def q_dve(e, ch):
            e.wait_ge(n_free, 1)
            e.wait_ge(q_scaled, 1)
            for gp in range(2):
                for a in range(2):
                    rows_ = slice(a * HD, a * HD + HD)
                    dst = qz[rows_, gp].rearrange("p b n -> p (b n)")
                    c0 = 8 * gp + 4 * a
                    for r in range(4):
                        ch.step(e.tensor_copy(dst[:, c0 + r:c0 + r + 7 * (P + NH) + 1:P + NH],
                                              pt[rows_, T_Q + gp * 4 + r, SEQ:NT]))
                ch.step(e.tensor_copy(ksn[:, gp, :], pt[:, T_KS + gp, SEQ:NT]))
            ch.settle()
            e.tensor_copy(swapm[:, 0:HD], ident[:, HD:P])
            e.tensor_copy(swapm[:, HD:P], ident[:, 0:HD]).then_inc(n_q.sem, 1)

        def smp_dve(e, ch):
            e.wait_ge(*nc_s(1))
            e.tensor_reduce(smax[:, 0:1], PS[:, 3, 0:NCMP_S], AX.X, ALU.max, negate=True).then_inc(nc_max.sem, 1)
            e.wait_ge(nc_exp, 1)
            ch.step(e.reciprocal(srec[:, 0:1], sden[:, 0:1]))
            ch.settle()
            e.tensor_scalar(pn[:, 0:NCMP_S], pn[:, 0:NCMP_S], srec[:, 0:1], None, ALU.mult).then_inc(nc_p.sem, 1)
            e.wait_ge(*nc_p(1))
            e.wait_ge(n_gate, 16)
            e.tensor_scalar(pg[:, 0:NCMP_S], pn[:, 0:NCMP_S], gbh[:, 0:1], None, ALU.mult).then_inc(nc_p.sem, 1)
            e.wait_ge(*nc_T(1))
            e.tensor_copy(pnT[0:NCMP_S, :], PS[0:NCMP_S, 5, 0:P]).then_inc(nc_Tc.sem, 1)
            e.tensor_copy(pgT[0:NCMP_S, :], PS[0:NCMP_S, 5, P:2 * P]).then_inc(nc_Tc.sem, 1)
            e.wait_ge(*n_imp(1))
            e.tensor_copy(imp1[:], PS[:, 7, 0:17]).then_inc(n_imp1.sem, 1)
            e.wait_ge(*n_imp(2))
            ch.step(e.tensor_copy(imp[:], PS[:, 7, 32:49]))
            ch.settle()
            ch.step(e.memset(imp[:, 0:1], 1.0e4))
            ch.step(e.memset(imp[:, 15:17], 1.0e4))
            ch.settle()
            ch.step(e.tensor_reduce(smn[:, 0:1], imp[:], AX.X, ALU.min))
            ch.settle()
            ch.step(e.scalar_tensor_tensor(out=eqb[:], in0=imp[:], scalar=smn[:, 0:1], in1=blk_no[:],
                                           op0=ALU.is_equal, op1=ALU.mult))
            ch.settle()
            ch.step(e.tensor_reduce(smn[:, 1:2], eqb[:], AX.X, ALU.max))
            ch.settle()
            e.tensor_scalar(dropadd[:], blk_no[:], smn[:, 1:2], NEG, ALU.is_equal, ALU.mult).then_inc(n_drop.sem, 1)
            smp_copy(e, 1, lambda a, b: e.tensor_copy(a, b), n_ev_d, lambda b: ssd_prep_dve(e, ch, b))
            e.wait_ge(n_sc, NB)
            e.tensor_reduce(smax[:, 2:3], PS[:, 4, :], AX.X, ALU.max, negate=True).then_inc(n_max.sem, 1)
            e.wait_ge(*n_drop(1))
            for h in range(2):
                ch.step(e.tensor_tensor(
                    pr_s[:, h * 512:h * 512 + 512].rearrange("p (j k n) -> p j k n", j=4, n=8),
                    PS[:, h, :].rearrange("p (j k n) -> p j k n", j=4, n=8),
                    dropadd[:, 0:16].unsqueeze(1).unsqueeze(3).to_broadcast([P, 4, 16, 8]), ALU.add))
            ch.step(e.tensor_copy(pr_s[:, 1024:1025], PS[:, 2, 0:1]))
            ch.settle()
            e.tensor_reduce(smax[:, 1:2], pr_s[:, 0:1025], AX.X, ALU.max, negate=True).then_inc(n_max.sem, 1)
            e.wait_ge(n_exp, 2)
            ch.step(e.reciprocal(srec[:, 1:3], sden[:, 1:3]))
            ch.settle()
            ch.step(e.tensor_tensor(sfac[:, 1:3], srec[:, 1:3], gbh[:, 1:3], ALU.mult))
            ch.settle()
            e.tensor_scalar(pr_w[:], pr_w[:], sfac[:, 2:3], None, ALU.mult).then_inc(n_pd.sem, 1)
            e.tensor_scalar(pr_s[:, 0:1025], pr_s[:, 0:1025], sfac[:, 1:2], None, ALU.mult).then_inc(n_pd.sem, 1)
            e.wait_ge(*n_pd(2))
            e.tensor_scalar(diag_n[:], ident[:], pr_s[:, 1024:1025], None, ALU.mult).then_inc(n_pd.sem, 1)
            e.wait_ge(n_pT, 1)
            e.tensor_copy(pT_w[:].rearrange("p y n -> p (y n)"), PS[:, 7, :]).then_inc(n_pTc, 1)
            e.tensor_copy(pnz[:], PS[0:NB, 3, 0:P]).then_inc(n_pTc, 1)
            for x in range(1, NB, 2):
                e.wait_ge(n_v, x + 1)
                bank = PV_ORDER[x] // 2
                e.tensor_copy(o_t[:, 2 * bank:2 * bank + 2, :].rearrange("p b n -> p (b n)"),
                              PS[0:NH, bank, :]).then_inc(n_oc.sem, 1)
            e.wait_ge(n_oT, 1)
            for gp in range(2):
                e.tensor_copy(o_s[:].rearrange("p (b h) -> p b h", h=NH)[:, :, 8 * gp:8 * gp + 8],
                              PS[:, 4 + gp, 0:P].rearrange("p (b h) -> p b h", h=NH)[:, :, 8 * gp:8 * gp + 8])\
                 .then_inc(n_o.sem, 1)
            e.wait_ge(*n_o(2))
            e.wait_ge(n_sw, 1)
            for half in range(2):
                for a in range(2):
                    src = (o_s[:] if a == half else PS[:, 1, 0:P])[half * HD:half * HD + HD, :]
                    for gp in range(2):
                        c0 = 8 * gp + 4 * a + half
                        e.tensor_copy(
                            mixf[half * HD:half * HD + HD, 4 * gp + 2 * a:4 * gp + 2 * a + 2, SEQ:NT],
                            src.rearrange("p (b h) -> p h b", h=NH)[:, c0:c0 + 3:2, :]).then_inc(n_mix.sem, 1)

        NC = SEQ // P
        R = slice(DT0, DT0 + NH)
        xa = pt[:, T_X:T_X + 12, :]
        c_tmp = at("c_tmp", [P, 2, NT], A0 + 8 * TILE)
        xdt = at("xdt", [P, NC, DI], A2 + 24960)
        st = at("st", [P, NC, DI], M_RING)
        cst = at("cst", [3 * NB, CONV_DIM], A0 + 8 * TILE)
        b_tok = at("b_tok", [P, NC, NG * DS], M_RING + 16384)
        cbm = at("cbm", [P, NG, NC, P], M_RING + 20480)
        xdte = at("xdte", [P, DI], M_RING + 24576)
        sel_h = at("sel_h", [P, NH, P], MF)
        sel_p = at("sel_p", [P, 8, P], MF + 8192)
        acs = at("acs", [P, SEQ], MF + 12288)
        dd = at("dd", [P, 16], MF + 14368)
        dta = at("dta", [P, NC, 2, NH], MF + 14432)
        te = at("te", [P, NC, NH], MF + 14944)
        dcb = at("dcb", [P, NC, NH], MF + 15200)
        aet = at("aet", [P, NC, NH], MF + 15456)
        HS = 3
        dec = at("dec", [P, HS, SEQ], A1)
        ebc = at("ebc", [P, HS, SEQ], A1 + 6144)
        ce = at("ce", [P, HS, SEQ], A1 + 12288)
        SPREAD_BANK = (0, 1, 6)
        sp = [at(f"sp{n}", [P, NT], A0 + 8 * TILE + 6144 + TILE * n) for n in range(5)]
        XR = A2 + 16384
        st_s = at("st_s", [P, 2, 8, DS], A1 + 18432)
        bcs = at("bcs", [P, 2, 4, DS], A1 + 26624)
        tmp_s = at("tmp_s", [P, 8, DS], XR)
        diag_b = at("diag_b", [P, 4, DS], XR + 4096)
        xprev = at("xprev", [P, 12, NB, 3], A1 + 30720)
        ddb = at("ddb", [P, 8, 16], XR + 6144)
        xds = at("xds", [P, 8, NB], XR + 6656)
        ys = at("ys", [P, 8, NB], XR + 6912)
        diag_e = at("diag_e", [P, NC, NH], A1 + 32896)
        so = at("so", [P, 8, DS], A1 + 12288)
        ssm_rms = at("ssm_rms", [P, 2, NT], A2 + (T_X + 8) * TILE)

        d_cld, d_selv = (
            sem(n) for n in ("d_cld", "d_selv"))
        d_xdte, d_stc = (
            sem(n) for n in ("d_xdte", "d_stc"))
        h_bc, h_min, h_ebc, h_dec, h_m, h_ce, h_y, h_out = (
            sem(n) for n in ("h_bc", "h_min", "h_ebc", "h_dec", "h_m", "h_ce", "h_y", "h_out"))
        e_diag, e_bc, e_bcs, e_new, e_rd, e_y = (
            sem(n) for n in ("e_diag", "e_bc", "e_bcs", "e_new", "e_rd", "e_y"))
        e_dec = sem("e_dec")
        e_ld, e_st = ([sem(f"{n}{x}") for x in range(2)] for n in ("e_ld", "e_st"))
        f_out = sem("f_out")

        def ssd_sp(e):
            x_again(e, 0)
            x_again(e, 1)
            for b in range(NB):
                if b == 2:
                    x_again(e, 2)
                if b >= 2:
                    e.wait_ge(e_st[b % 2], 16 * (b // 2))
                    e.wait_ge(e_rd, b - 1)
                e.dma_start(st_s[:, b % 2], i["state_ssm"][0, b].rearrange("(k h) p n -> (h p) k n", h=2))\
                 .then_inc(e_ld[b % 2], 16)
                if b:
                    store_state(e, b - 1)
            x_again(e, 3)
            store_state(e, NB - 1)
            e.wait_ge(*f_so(2))
            e.dma_start(o["ssm_p"][0, 0].rearrange("(k h) p n -> (h p) k n", h=2), so[:]).then_inc(f_out, 16)
            for x in range(2):
                e.wait_ge(e_st[x], 16 * NB // 2)
            e.wait_ge(f_out, 16)

        def store_state(e, b):
            e.wait_ge(e_new, b + 1)
            e.dma_start(o["ssm_s"][0, b].rearrange("(k h) p n -> (h p) k n", h=2), st_s[:, b % 2]).then_inc(e_st[b % 2], 16)

        def ssd_pool(e, ch):
            e.wait_ge(n_v, NB)
            ch.step(e.memset(sel_h[:], 1.0))
            ch.step(e.memset(sel_p[:], 1.0))
            ch.settle()
            e.affine_select(out=sel_h[R], in_=sel_h[R], compare_op=ALU.is_equal, fill=0.0, base=0,
                            pattern=[[-1, NH], [0, P]], channel_multiplier=1).then_inc(d_selv, 1)
            e.affine_select(out=sel_p[R].rearrange("p k (a n) -> p k a n", a=2),
                            in_=sel_p[R].rearrange("p k (a n) -> p k a n", a=2), compare_op=ALU.is_equal,
                            fill=0.0, base=0, pattern=[[-2, 8], [-1, 2], [0, HD]],
                            channel_multiplier=1).then_inc(d_selv, 1)
            e.wait_ge(e_diag, 1)
            for h in range(NH):
                if h % 2 == 0:
                    b = h // 2
                    e.wait_ge(e_ld[b % 2], 16 * (b // 2 + 1))
                    s = st_s[:, b % 2]
                    e.tensor_tensor(s, s, ddb[:, :, NB + b:NB + b + 1].to_broadcast([P, 8, DS]), ALU.mult)\
                     .then_inc(e_dec, 1)
                e.wait_ge(h_ebc, h + 1)
                if h >= HS:
                    e.wait_ge(h_y, h + 1 - HS)
                e.tensor_tensor(ce[:, h % HS], ebc[:, h % HS], xa[:, 10 + h // 8, 0:SEQ], ALU.mult).then_inc(h_ce, 1)

        def ssd_prep_dve(e, ch, b):
            if b == 0:
                e.wait_ge(*d_ct(1))
                e.tensor_copy(xprev[:].rearrange("p k b w -> p (k b w)"), PS[:, 2, P:P + 288]).then_inc(d_xp.sem, 1)
                e.wait_ge(*d_xp(1))
                dt_dve(e, ch)
            else:
                for k in CONV_AT[b]:
                    conv(e, ch, k)

        CONV_AT = [(), (0, 1), (2, 3), (4, 5), (6, 7), (8, 9), (10,), (11,)]

        def dt_dve(e, ch):
            x, na, ex, u, l = (sp[n][R, :] for n in range(5))
            ch.step(e.tensor_scalar(x, pt[R, T_GD, :], hpar[R, 0:1], None, ALU.add))
            ch.settle()
            e.scalar_tensor_tensor(out=na, in0=x, scalar=-1.0, in1=x, op0=ALU.mult, op1=ALU.min).then_inc(d_e.sem, 1)
            e.wait_ge(*d_u(1))
            e.tensor_scalar(u, ex, 1.0, None, ALU.add).then_inc(d_e.sem, 1)
            e.wait_ge(*d_e(2))
            ch.step(e.tensor_scalar(na, u, -1.0, None, ALU.add))
            ch.settle()
            ch.step(e.tensor_tensor(na, ex, na, ALU.subtract))
            e.wait_ge(*d_ln(2))
            ch.settle()
            ch.step(e.reciprocal(ex, u))
            ch.settle()
            ch.step(e.tensor_tensor(na, na, ex, ALU.mult))
            ch.settle()
            ch.step(e.tensor_tensor(l, l, na, ALU.add))
            ch.settle()
            dt = pt[R, T_GD, :]
            ch.step(e.scalar_tensor_tensor(out=dt, in0=x, scalar=0.0, in1=l, op0=ALU.max, op1=ALU.add))
            ch.step(e.tensor_scalar(hpar[R, 2:3], hpar[R, 3:4], -1.0, None, ALU.mult))
            ch.settle()
            a = sp[0][R, :]
            ch.step(e.tensor_scalar(a, dt, hpar[R, 2:3], None, ALU.mult))
            ch.step(e.memset(sp[1][R, :], 1.0))
            ch.step(e.tensor_copy(dd[R, 0:NB], dt[:, SEQ:NT]))
            ch.settle()
            for c in range(NC):
                e.tensor_tensor_scan(acs[R, c * P:c * P + P], sp[1][R, 0:P], a[:, c * P:c * P + P], 0.0,
                                     ALU.mult, ALU.add).then_inc(d_acs.sem, 1)
            e.wait_ge(*d_acs(NC))
            for c in range(NC):
                e.tensor_scalar(diag_e[R, c, :], ident[R, R], acs[R, c * P + P - 1:c * P + P], None,
                                ALU.mult).then_inc(d_diag.sem, 1)
        def conv(e, ch, k):
            xr, out = pt[:, T_X + k, :], c_tmp[:, k % 2, :]
            w = [pcol[:, R_CW + 12 * y + k:R_CW + 12 * y + k + 1] for y in range(4)]
            if k >= 2:
                e.wait_ge(*d_xa(k - 1))
            ch.step(e.tensor_scalar(out, xr, w[3], None, ALU.mult))
            for y in (2, 1, 0):
                ch.settle()
                d = 3 - y
                e.scalar_tensor_tensor(out=out[:, d:SEQ], in0=xr[:, 0:SEQ - d], scalar=w[y], in1=out[:, d:SEQ],
                                       op0=ALU.mult, op1=ALU.add)
                last = e.scalar_tensor_tensor(out=out[:, SEQ:NT], in0=xprev[:, k, :, y], scalar=w[y],
                                              in1=out[:, SEQ:NT], op0=ALU.mult, op1=ALU.add)
                if y:
                    ch.step(last)
            last.then_inc(d_conv.sem, 1)

        def ssd_dve(e, ch):
            e.wait_ge(*d_T(1))
            e.tensor_copy(dta[:].rearrange("p c x h -> p (c x h)"), PS[:, 0, 0:P]).then_inc(d_dta.sem, 1)
            e.wait_ge(*d_dta(1))
            e.wait_ge(*d_T(2))
            e.wait_ge(*d_te(1))
            e.tensor_tensor(aet[:], PS[:, 1, 0:64].rearrange("p (c h) -> p c h", h=NH), dta[:, :, 1, :],
                            ALU.subtract).then_inc(d_ae.sem, 1)
            for f in range(2 * NC):
                c, half = f // 2, f % 2
                e.wait_ge(*d_xT(f + 1))
                e.tensor_tensor(xdt[:, c, half * 512:half * 512 + 512].rearrange("p (h d) -> p h d", d=HD),
                                PS[:, 2 + f % 2, :].rearrange("p (h d) -> p h d", d=HD),
                                dta[:, c, 0, 8 * half:8 * half + 8].unsqueeze(2).to_broadcast([P, 8, HD]),
                                ALU.mult).then_inc(d_xdt.sem, 1)
            for g in range(NG):
                e.wait_ge(*d_cb(g + 1))
                e.tensor_tensor(cbm[:, g], PS[:, 6 + g, :].rearrange("p (c l) -> p c l", l=P),
                                causT[:].unsqueeze(1).to_broadcast([P, NC, P]), ALU.mult).then_inc(d_cbm.sem, 1)
            e.wait_ge(*d_xdt(2 * NC))
            e.wait_ge(*d_te(2))
            for c in range(NC):
                if c:
                    e.wait_ge(*d_st(2 * c))
                e.tensor_tensor(xdte[:].rearrange("p (h d) -> p h d", d=HD), xdt[:, c].rearrange("p (h d) -> p h d", d=HD),
                                te[:, c, :].unsqueeze(2).to_broadcast([P, NH, HD]), ALU.mult).then_inc(d_xdte, 1)
                if c:
                    ch.step(e.tensor_tensor(st[:, c].rearrange("p (h d) -> p h d", d=HD),
                                            st[:, c - 1].rearrange("p (h d) -> p h d", d=HD),
                                            dcb[:, c, :].unsqueeze(2).to_broadcast([P, NH, HD]), ALU.mult))
                    ch.settle()
                for g in range(NG):
                    e.wait_ge(*d_st(2 * c + g + 1))
                    dst = st[:, c, g * 512:g * 512 + 512]
                    if c:
                        ins = e.tensor_tensor(dst, dst, PS[:, 2 + g, :], ALU.add)
                    else:
                        ins = e.tensor_copy(dst, PS[:, 2 + g, :])
                    ins.then_inc(d_stc, 1)
                e.wait_ge(d_stc, 2 * (c + 1))
            def lower(h):
                e.wait_ge(h_bc, h + 1)
                if h >= HS:
                    e.wait_ge(h_y, h + 1 - HS)
                for c in range(NC):
                    last = e.tensor_scalar(dec[:, h % HS, c * P:c * P + P], PS[:, SPREAD_BANK[h % HS], c * P:c * P + P],
                                           dta[:, c, 1, h:h + 1], 0.0, ALU.subtract, ALU.min)
                last.then_inc(h_min, 1)
            for h in range(HS - 1):
                lower(h)
            step_first(e, ch)
            for h in range(NH):
                if h % 2 == 0:
                    step_diag(e, h // 2)
                    if h:
                        step_read(e, h // 2 - 1)
                e.wait_ge(h_dec, h + 1)
                e.tensor_tensor(dec[:, h % HS], dec[:, h % HS], cbm[:, h // 8].rearrange("p c l -> p (c l)"),
                                ALU.mult).then_inc(h_m, 1)
                if h + HS - 1 < NH:
                    lower(h + HS - 1)
                if h % 2:
                    if h > 1:
                        pair_out(e, h // 2 - 1)
                    step_state(e, ch, h // 2)
            step_read(e, NB - 1)
            pair_out(e, 7)
            step_last(e, ch)

        def pair_out(e, k):
            e.wait_ge(h_y, 2 * k + 2)
            e.scalar_tensor_tensor(out=mixf[:, 8 + k, 0:SEQ], in0=xa[:, k, 0:SEQ], scalar=dskip[:, k:k + 1],
                                   in1=PS[:, 4 + k % 2, :], op0=ALU.mult, op1=ALU.add).then_inc(h_out, 1)

        def ssd_prep_act(e, b):
            if b == 0:
                e.wait_ge(*d_e(1))
                e.activation(sp[2][R, :], sp[1][R, :], ACT.Exp).then_inc(d_u.sem, 1)
                e.activation(hpar[R, 3:4], hpar[R, 1:2], ACT.Exp).then_inc(d_ln.sem, 1)
                e.wait_ge(*d_e(2))
                e.activation(sp[4][R, :], sp[3][R, :], ACT.Ln).then_inc(d_ln.sem, 1)
            elif b == 1:
                e.wait_ge(*d_acs(NC))
                e.activation(dd[R, NB:2 * NB], sp[0][R, SEQ:NT], ACT.Exp).then_inc(e_dd.sem, 1)
            if b:
                for k in CONV_AT[b]:
                    e.wait_ge(*d_conv(k + 1))
                    e.activation(xa[:, k, :], c_tmp[:, k % 2, :], ACT.Silu,
                                 bias=pcol[:, R_CB + k:R_CB + k + 1]).then_inc(d_xa.sem, 1)

        def ssd_act(e, ch):
            for k in range(8):
                e.activation(pt[:, T_Z + k, :], pt[:, T_Z + k, :], ACT.Silu).then_inc(f_z.sem, 1)
            e.wait_ge(*d_T(2))
            e.activation(dcb[:], PS[:, 1, 0:64].rearrange("p (c h) -> p c h", h=NH), ACT.Exp).then_inc(d_te.sem, 1)
            e.wait_ge(*d_ae(1))
            e.activation(te[:], aet[:], ACT.Exp).then_inc(d_te.sem, 1)
            for f in range(2):
                e.wait_ge(*d_bT(f + 1))
                e.activation(b_tok[:, 2 * f:2 * f + 2, :].rearrange("p c n -> p (c n)"), PS[:, 4 + f, :],
                             ACT.Copy).then_inc(d_btok.sem, 1)
            for h in range(NH):
                e.wait_ge(h_min, h + 1)
                if h >= HS:
                    e.wait_ge(h_ce, h + 1 - HS)
                e.activation(ebc[:, h % HS], PS[:, SPREAD_BANK[h % HS], :], ACT.Exp).then_inc(h_ebc, 1)
                e.activation(dec[:, h % HS], dec[:, h % HS], ACT.Exp).then_inc(h_dec, 1)
                if h % 2:
                    step_act(e, h // 2)

        def ssd_pe(e):
            e.wait_ge(*n_mix(8))
            e.wait_ge(*d_acs(NC))
            for c in range(NC):
                e.transpose(PS[:, 0, c * 32:c * 32 + 16], pt[R, T_GD, c * P:c * P + P], ident[R, R])
                last = e.transpose(PS[:, 0, c * 32 + 16:c * 32 + 32], acs[R, c * P:c * P + P], ident[R, R])
            last.then_inc(d_T.sem, 1)
            e.wait_ge(*d_diag(NC))
            e.matmul(PS[:, 1, 0:64], ones[R, :], diag_e[R].rearrange("p c h -> p (c h)"), start=True,
                     stop=True).then_inc(d_T.sem, 1)
            for f in range(2 * NC):
                c, half = f // 2, f % 2
                e.wait_ge(*d_xa(4 * half + 4))
                if f >= 2:
                    e.wait_ge(*d_xdt(f - 1))
                for x in range(4):
                    last = e.transpose(PS[:, 2 + f % 2, x * P:x * P + P], xa[:, 4 * half + x, c * P:c * P + P], ident[:])
                last.then_inc(d_xT.sem, 1)
            e.wait_ge(*d_xa(12))
            for f in range(2):
                for x in range(4):
                    last = e.transpose(PS[:, 4 + f, x * P:x * P + P],
                                       xa[:, 8 + x % 2, (2 * f + x // 2) * P:(2 * f + x // 2) * P + P], ident[:])
                last.then_inc(d_bT.sem, 1)
            e.wait_ge(*d_xp(1))
            for g in range(NG):
                for c in range(NC):
                    last = e.matmul(PS[:, 6 + g, c * P:c * P + P], xa[:, 8 + g, c * P:c * P + P],
                                    xa[:, 10 + g, c * P:c * P + P], start=True, stop=True)
                last.then_inc(d_cb.sem, 1)
            e.wait_ge(*d_btok(2))
            e.wait_ge(*d_xdt(2 * NC))
            for c in range(NC):
                e.wait_ge(d_xdte, c + 1)
                for g in range(NG):
                    if c:
                        e.wait_ge(d_stc, 2 * c)
                    e.matmul(PS[:, 2 + g, :], b_tok[:, c, g * DS:g * DS + DS], xdte[:, g * 512:g * 512 + 512],
                             start=True, stop=True).then_inc(d_st.sem, 1)
            e.wait_ge(d_selv, 2)
            e.wait_ge(*d_ae(1))
            e.wait_ge(*d_cbm(2))

            def spread(h):
                if h >= HS:
                    e.wait_ge(h_ebc, h + 1 - HS)
                e.matmul(PS[:, SPREAD_BANK[h % HS], :], sel_h[R, h, :], acs[R, :], start=True, stop=True).then_inc(h_bc, 1)

            for h in range(HS - 1):
                spread(h)
            e.wait_ge(*e_dd(1))
            for k in range(8):
                last = e.matmul(PS[:, 7, 16 * k:16 * k + 16], sel_p[R, k, :], dd[R, :], start=True, stop=True)
            last.then_inc(e_bc, 1)
            for h in range(NH):
                if h + HS - 1 < NH:
                    spread(h + HS - 1)
                if h % 2:
                    step_pe(e, h // 2)
                e.wait_ge(h_m, h + 1)
                e.wait_ge(h_ce, h + 1)
                if h == 0:
                    e.wait_ge(d_stc, 2 * NC)
                k = h // 2
                if k >= 2:
                    e.wait_ge(h_out, k - 1)
                for c in range(NC):
                    out = PS[(h % 2) * HD:(h % 2) * HD + HD, 4 + k % 2, c * P:c * P + P]
                    hs = slice(h * HD, h * HD + HD)
                    last = e.matmul(out, xdt[:, c, hs], dec[:, h % HS, c * P:c * P + P], start=True, stop=(c == 0))
                    if c:
                        last = e.matmul(out, st[:, c - 1, hs], ce[:, h % HS, c * P:c * P + P], start=False, stop=True)
                last.then_inc(h_y, 1)

        def step_pe(e, b):
            e.wait_ge(e_diag, b + 1)
            if b >= 2:
                e.wait_ge(e_bcs, b - 1)
            e.matmul(PS[:, 2 + b % 2, :], ones[:], diag_b[:].rearrange("p x n -> p (x n)"), start=True,
                     stop=True).then_inc(e_bc, 1)

        def step_act(e, b):
            e.wait_ge(e_bc, b + 2)
            if b >= 2:
                e.wait_ge(e_y, b - 1)
            e.activation(bcs[:, b % 2].rearrange("p x n -> p (x n)"), PS[:, 2 + b % 2, :],
                         ACT.Copy).then_inc(e_bcs, 1)

        def step_first(e, ch):
            e.wait_ge(e_bc, 1)
            ch.step(e.tensor_copy(ddb[:].rearrange("p k x -> p (k x)"), PS[:, 7, 0:P]))
            ch.settle()
            ch.step(e.tensor_tensor(xds[:], xa[:, 0:8, SEQ:NT], ddb[:, :, 0:NB], ALU.mult))
            ch.settle()

        def step_diag(e, b):
            if b:
                e.wait_ge(e_bc, b + 1)
            e.tensor_tensor(diag_b[:], ident[:].unsqueeze(1).to_broadcast([P, 4, P]),
                            xa[:, 8:12, SEQ + b:SEQ + b + 1].to_broadcast([P, 4, P]), ALU.mult).then_inc(e_diag, 1)

        def step_state(e, ch, b):
            grouped = lambda ap: ap.rearrange("p (g k) n -> p g k n", g=NG)
            s = st_s[:, b % 2]
            e.wait_ge(e_bcs, b + 1)
            ch.step(e.tensor_tensor(grouped(tmp_s[:]), bcs[:, b % 2, 0:2, :].unsqueeze(2).to_broadcast([P, NG, 4, DS]),
                                    grouped(xds[:, :, b:b + 1].to_broadcast([P, 8, DS])), ALU.mult))
            ch.settle()
            e.wait_ge(e_dec, b + 1)
            e.tensor_tensor(s, s, tmp_s[:], ALU.add).then_inc(e_new, 1)

        def step_read(e, b):
            grouped = lambda ap: ap.rearrange("p (g k) n -> p g k n", g=NG)
            s = st_s[:, b % 2]
            e.wait_ge(e_new, b + 1)
            e.tensor_tensor(grouped(tmp_s[:]), grouped(s), bcs[:, b % 2, 2:4, :].unsqueeze(2).to_broadcast([P, NG, 4, DS]),
                            ALU.mult).then_inc(e_rd, 1)
            e.wait_ge(e_rd, b + 1)
            e.tensor_reduce(ys[:, :, b], tmp_s[:], AX.X, ALU.add).then_inc(e_y, 1)

        def step_last(e, ch):
            e.wait_ge(e_y, NB)
            for k in range(8):
                ch.step(e.scalar_tensor_tensor(out=mixf[:, 8 + k, SEQ:NT], in0=xa[:, k, SEQ:NT],
                                               scalar=dskip[:, k:k + 1], in1=ys[:, k, :], op0=ALU.mult, op1=ALU.add))
            ch.settle()

        def ssd_end_pe(e):
            e.wait_ge(d_stc, 2 * NC)
            e.wait_ge(h_ebc, NH)
            for k in range(8):
                last = e.transpose(PS[:, k // 4, (k % 4) * P:(k % 4) * P + P], st[:, NC - 1, k * P:k * P + P], ident[:])
                if k % 4 == 3:
                    last.then_inc(f_T.sem, 1)
            e.wait_ge(h_out, 8)
            e.wait_ge(xr_ld, 16 * 5)
            e.wait_ge(*f_so(2))
            for k in range(8):
                turn_x(e, 2 * k)
                turn_x(e, 2 * k + 1)
                e.wait_ge(*f_sq(k + 1))
                g = k // 4
                for h in range(2):
                    last = e.matmul(PS[:, 4 + 2 * g + h, 0:HN], ones[:], sqb[:, k % 2, h * HN:h * HN + HN],
                                    start=(k % 4 == 0), stop=(k % 4 == 3))
                last.then_inc(f_sum.sem, 1)
            turn_x(e, KT)

        sqb = at("sqb", [P, 2, NT], A1)

        def ssd_end_act(e, ch):
            for x in range(2):
                e.wait_ge(*f_T(x + 1))
                e.activation(so[:, 4 * x:4 * x + 4, :].rearrange("p k n -> p (k n)"), PS[:, x, :],
                             ACT.Copy).then_inc(f_so.sem, 1)
            for k in range(8):
                e.wait_ge(*f_g(k + 1))
                if k >= 2:
                    e.wait_ge(*f_sum(k - 1))
                e.activation(sqb[:, k % 2, :], mixf[:, 8 + k, :], ACT.Square).then_inc(f_sq.sem, 1)
                for x in (2 * k, 2 * k + 1):
                    if 4 < x < 12:
                        e.wait_ge(*f_g(x - 3))
                    take_x(e, x)
            take_x(e, KT)
            e.wait_ge(f_out, 16)
            for x in range(2):
                e.wait_ge(e_st[x], 16 * NB // 2)
            e.wait_ge(*f_sum(8))
            for k in range(8):
                mix_high(e, k)

        def norm_rms(e, g):
            e.activation(ssm_rms[:, g].rearrange("p (h n) -> p h n", h=2), PS[:, 4 + 2 * g:6 + 2 * g, 0:HN],
                         ACT.Sqrt, scale=1.0 / (DI // NG), bias=eps_col[:]).then_inc(f_rms.sem, 1)

        def ssd_end_dve(e, ch):
            for k in range(8):
                e.wait_ge(*f_z(k + 1))
                e.tensor_tensor(mixf[:, 8 + k, :], mixf[:, 8 + k, :], pt[:, T_Z + k, :], ALU.mult).then_inc(f_g.sem, 1)

        def normed_groups(e, ch, g):
            e.wait_ge(*f_rms(g + 1))
            ch.step(e.reciprocal(ssm_rms[:, g], ssm_rms[:, g]))
            ch.settle()
            for k in range(4 * g, 4 * g + 4):
                e.scalar_tensor_tensor(out=mixf[:, 8 + k, :], in0=mixf[:, 8 + k, :],
                                       scalar=pcol[:, R_SSMN + k:R_SSMN + k + 1], in1=ssm_rms[:, g],
                                       op0=ALU.mult, op1=ALU.mult).then_inc(f_mix.sem, 1)

        x_r = [at(f"x_r{t}", [P, D_MODEL], off) for t, off in enumerate((A2, A2 + 8192, M_RING + 24576, MF))]
        xs_r = at("xs_r", [4 * NB, D_MODEL // 4], A2 + T_GD * TILE)
        x_acc = at("x_acc", [P, KT, 2, HN], A3)
        xf = x_acc[:].rearrange("p t h n -> p t (h n)")
        mix_hi = at("mix_hi", [P, KT, NT], A1, F32R)
        mix_lo = at("mix_lo", [P, KT, NT], A2, F32R)
        h2_hi = at("h2_hi", [P, KT, NT], A4, F32R)
        h2_lo = at("h2_lo", [P, KT, NT], A0, F32R)
        ssq_a = at("ssq_a", [P, NT], 4096)
        sq2 = at("sq2", [P, 2, NT], 4096 + TILE)
        u_hi = at("u_hi", [P, FC // P, NT], A1, F32R)
        u_lo = at("u_lo", [P, FC // P, NT], A1 + FC // P * TILE, F32R)
        relu = at("relu", [P, 2, 2, HN], A2)
        sqr = at("sqr", [P, 2, NT], A2 + 2 * TILE)
        y_0 = at("y_0", [P, KT, NT], A4)
        y_out = at("y_out", [P, 4, D_MODEL], A0)
        ys_out = at("ys_out", [NB, D_MODEL], A2 + 16384)

        xr_ld = sem("xr_ld")
        r_pe, r_acc, m_hi, m_lo, o_hi, o_lo, o_sq, o_sum, o_pe, o_rms, o_rstd = (
            sem(n) for n in ("r_pe", "r_acc", "m_hi", "m_lo", "o_hi", "o_lo", "o_sq", "o_sum", "o_pe", "o_rms",
                             "o_rstd"))
        G_OUT0 = NTILE
        G_MLP0 = G_OUT0 + KT
        G_CHUNK = FC // P + KT
        w_o, w_u, w_d = i["w_out"][0], i["w_up"][0], i["w_down"][0]

        def x_again(e, t):
            if t == 2:
                e.wait_ge(*d_st(2 * NC))
                e.dma_start(xs_r[:], i["x_sample"].rearrange("b t (q n) -> (b t q) n", q=4)).then_inc(xr_ld, 16)
            elif t == 3:
                e.wait_ge(h_bc, NH)
            e.dma_start(x_r[t][:], i["x_prompt"][0, t * P:t * P + P, :]).then_inc(xr_ld, 16)

        def out_sp(e):
            e.wait_ge(*f_T(2))
            for blk in range(OUT_BLOCKS):
                for kp in range(4):
                    n = OUT0 + 4 * blk + kp
                    src = pair_src(w_o, kp * PK, slice(blk * PN, blk * PN + PN))
                    load_piece(e, n, n, [(w_raw[:, n % N_RAW, 2 * y:2 * y + 2, :], src[y]) for y in range(2)])

        def out_pe(e):
            e.wait_ge(r_acc, KT + 1)
            for blk in range(OUT_BLOCKS):
                if blk >= 2:
                    e.wait_ge(g_out, G_OUT0 + 2 * (blk - 1))
                for kp in range(4):
                    n = OUT0 + 4 * blk + kp
                    if blk == 0:
                        e.wait_ge(m_lo, PK * (kp + 1))
                    elif (blk, kp) == (1, 0):
                        e.wait_ge(*f_rms(2))
                    mul_piece(e, n, n, 4 * (blk % 2), mix_hi, mix_lo, kp * PK, kp == 0, kp == 3)
            e.wait_ge(g_out, G_MLP0 - 2)
            e.wait_ge(o_sum, KT)
            for h in range(2):
                last = e.matmul(PS[:, h, 0:HN], ones[:], ssq_a[:, h * HN:h * HN + HN], start=True, stop=True)
            last.then_inc(o_pe, 1)

        def out_act(e):
            for n in range(2):
                hi_piece(e, OUT0 + n, n, OUT0 // 4 + 1)
            for g in range(NG):
                norm_rms(e, g)
            for k in range(8):
                e.wait_ge(*f_mix(k + 1))
                mix_high(e, 8 + k)
            for n in range(2, OUT_PIECES + 2):
                if n < OUT_PIECES + 1:
                    hi_piece(e, OUT0 + n, n, (OUT0 + n) // 4 + 1)
                if n >= 5 and n % 4 == 1:
                    normed_act(e, n // 4 - 1)
            hi_piece(e, MLP0 + 1, 1, MLP0 // 4 + 1)
            e.wait_ge(o_pe, 1)
            e.activation(rstd_bc[:], PS[:, 0:2, 0:HN], ACT.Sqrt, scale=1.0 / D_MODEL, bias=eps_col[:]).then_inc(o_rms, 1)

        def turn_x(e, k):
            if k >= 4:
                e.wait_ge(r_acc, k - 3)
            if k < KT:
                for t in range(4):
                    last = e.transpose(PS[:, k % 4, t * P:t * P + P], x_r[t][:, k * P:k * P + P], ident[:])
            else:
                for j in range(4):
                    last = e.transpose(PS[:, k % 4, j * 32:j * 32 + 32], xs_r[:, j * P:j * P + P], ident[0:32, 0:32])
            last.then_inc(r_pe, 1)

        def take_x(e, k):
            e.wait_ge(r_pe, k + 1)
            if k < KT:
                e.activation(xf[:, k, 0:SEQ], PS[:, k % 4, :], ACT.Copy).then_inc(r_acc, 1)
            else:
                for q in range(4):
                    last = e.activation(xf[:, 4 * q:4 * q + 4, SEQ:NT],
                                        PS[:, k % 4, 0:P].rearrange("p (j b q) -> p j b q", j=4, q=4)[:, :, :, q],
                                        ACT.Copy)
                last.then_inc(r_acc, 1)

        def mix_high(e, k):
            e.activation(mix_hi[:, k, :], mixf[:, k, :], ACT.Copy).then_inc(m_hi, 1)

        def mix_low(e, k):
            e.wait_ge(m_hi, k + 1)
            e.tensor_tensor(mix_lo[:, k, :], mixf[:, k, :], mix_hi[:, k, :].bitcast(F32), ALU.subtract).then_inc(m_lo, 1)

        def normed_act(e, blk):
            for k in (2 * blk, 2 * blk + 1):
                e.wait_ge(g_out, G_OUT0 + k + 1)
                e.activation(h2_hi[:, k, :], xf[:, k, :], ACT.Copy,
                             scale=pcol[:, R_LNMLP + k:R_LNMLP + k + 1]).then_inc(o_hi, 1)
                if k >= 2:
                    e.wait_ge(o_sum, k - 1)
                e.activation(sq2[:, k % 2, :], xf[:, k, :], ACT.Square).then_inc(o_sq, 1)

        def out_dve(e, ch):
            for k in range(8):
                mix_low(e, k)
            for n in range(2):
                lo_piece(e, OUT0 + n, n)
            for g in range(NG):
                normed_groups(e, ch, g)
            for k in range(8, KT):
                mix_low(e, k)
            for n in range(2, OUT_PIECES + 2):
                if n == OUT_PIECES + 1:
                    e.wait_ge(w_used, MLP0)
                else:
                    lo_piece(e, OUT0 + n, n)
                if n >= 5 and n % 4 == 1:
                    blk = n // 4 - 1
                    for m in range(2):
                        residual(e, 2 * blk + m, 4 * (blk % 2) + 2 * m)
                    for k in (2 * blk, 2 * blk + 1):
                        e.wait_ge(o_hi, k + 1)
                        e.scalar_tensor_tensor(out=h2_lo[:, k, :], in0=xf[:, k, :],
                                               scalar=pcol[:, R_LNMLP + k:R_LNMLP + k + 1],
                                               in1=h2_hi[:, k, :].bitcast(F32), op0=ALU.mult,
                                               op1=ALU.subtract).then_inc(o_lo, 1)
            lo_piece(e, MLP0 + 1, 1)
            e.wait_ge(o_rms, 1)
            e.reciprocal(rstd_bc[:], rstd_bc[:]).then_inc(o_rstd, 1)

        def residual(e, tile, bank):
            e.tensor_tensor(x_acc[:, tile], PS[:, bank:bank + 2, 0:HN], x_acc[:, tile], ALU.add).then_inc(g_out, 1)

        def out_pool(e):
            for k in range(KT):
                e.wait_ge(o_sq, k + 1)
                if k == 0:
                    e.tensor_copy(ssq_a[:], sq2[:, 0, :]).then_inc(o_sum, 1)
                else:
                    e.wait_ge(o_sum, k)
                    e.tensor_tensor(ssq_a[:], ssq_a[:], sq2[:, k % 2, :], ALU.add).then_inc(o_sum, 1)

        u_relu, u_sq, u_hi_rdy = (
            sem(n) for n in ("u_relu", "u_sq", "u_hi_rdy"))
        UP = UP_PIECES

        def mlp_sp(e):
            def chunk(c):
                n0 = c * CHUNK_PIECES + MLP0
                with e.Fori(0, UP_BLOCKS // 2) as it:
                    for z in range(8):
                        col = c * FC + it * (2 * PN) + (z // 4) * PN
                        src = pair_src(w_u, (z % 4) * PK, bass.ds(col, PN))
                        load_piece(e, n0 + it * 8 + z, z, [(w_raw[:, z % N_RAW, 2 * y:2 * y + 2, :], src[y])
                                                           for y in range(2)])
                with e.Fori(0, DOWN_BLOCKS // 2) as it:
                    for z in range(4):
                        col = it * (2 * PN) + (z // 2) * PN
                        parts = []
                        for y in range(2):
                            row = c * FC + ((z % 2) * PK + 2 * y) * P
                            parts.append((w_raw[:, z % N_RAW, 2 * y:2 * y + 2, :],
                                          w_d[bass.ds(row, 2 * P), bass.ds(col, PN)]
                                          .rearrange("(k p) n -> p k n", p=P)))
                        load_piece(e, n0 + it * 4 + (UP + z), z, parts)
            with e.Fori(0, N_CHUNK) as c:
                chunk(c)

        def mlp_pe(e):
            e.wait_ge(o_rms, 1)

            with e.Fori(0, N_CHUNK) as c:
                n0, g0 = c * CHUNK_PIECES + MLP0, c * G_CHUNK + G_MLP0
                with e.Fori(0, UP_BLOCKS // 2) as it:
                    for half in range(2):
                        e.wait_ge(g_out, g0 + it * 4 + (2 * half - 2))
                        for kp in range(4):
                            z = 4 * half + kp
                            e.wait_ge(o_lo, PK * (kp + 1))
                            mul_piece(e, n0 + it * 8 + z, z, 4 * half, h2_hi, h2_lo, kp * PK, kp == 0, kp == 3)
                with e.Fori(0, DOWN_BLOCKS // 2) as it:
                    for half in range(2):
                        e.wait_ge(g_out, g0 + it * 4 + (2 * half - 2 + FC // P))
                        for kp in range(2):
                            z = 2 * half + kp
                            e.wait_ge(g_out, g0 + 4 * (kp + 1))
                            mul_piece(e, n0 + it * 4 + (UP + z), z, 4 * half, u_hi, u_lo, kp * PK, kp == 0, kp == 1)

        def mlp_act(e):
            def chunk(c, last):
                n0, g0 = c * CHUNK_PIECES + MLP0, c * G_CHUNK + G_MLP0
                uses0 = c * (CHUNK_PIECES // 4) + (MLP0 // 4 + 1)
                with e.Fori(0, UP_BLOCKS // 2) as it:
                    for z in range(2, 10):
                        hi_piece(e, n0 + it * 8 + z, z, uses0 + it * 2 + z // 4)
                        if z in (5, 9):
                            for m in range(2):
                                squared(e, c, g0, it * 4 + (2 * (z // 9) + m), m)

                def down(it, zs):
                    for z in zs:
                        hi_piece(e, n0 + it * 4 + (UP + z), z, uses0 + it + (UP + z) // 4)
                        if last and z in (3, 5):
                            final_act(e, 2 * it + z // 5)
                if not last:
                    with e.Fori(0, DOWN_BLOCKS // 2) as it:
                        down(it, range(2, 6))
                else:
                    for it in range(DOWN_BLOCKS // 2):
                        down(it, range(2, 6 if it < DOWN_BLOCKS // 2 - 1 else 4))
                    final_act(e, DOWN_BLOCKS - 1)
            with e.Fori(0, N_CHUNK - 1) as c:
                chunk(c, False)
            chunk(N_CHUNK - 1, True)

        def squared(e, c, g0, tile, m):
            count = tile + c * (FC // P)
            e.wait_ge(u_relu, count + 1)
            e.wait_ge(g_out, tile + (g0 - 1))
            e.activation(sqr[:, m, :], relu[:, m].rearrange("p h n -> p (h n)"), ACT.Square).then_inc(u_sq, 1)
            e.wait_ge(u_sq, count + 1)
            e.activation(u_hi[:, tile, :], sqr[:, m, :], ACT.Copy).then_inc(u_hi_rdy, 1)

        def mlp_dve(e):
            def chunk(c, last):
                n0 = c * CHUNK_PIECES + MLP0
                with e.Fori(0, UP_BLOCKS // 2) as it:
                    for z in range(2, 10):
                        lo_piece(e, n0 + it * 8 + z, z)
                        if z in (5, 9):
                            for m in range(2):
                                bank = 4 * (z // 9) + 2 * m
                                e.scalar_tensor_tensor(out=relu[:, m], in0=PS[:, bank:bank + 2, 0:HN], scalar=0.0,
                                                       in1=rstd_bc[:], op0=ALU.max, op1=ALU.mult).then_inc(u_relu, 1)
                            for m in range(2):
                                tile = it * 4 + (2 * (z // 9) + m)
                                e.wait_ge(u_hi_rdy, tile + c * (FC // P) + 1)
                                e.tensor_tensor(u_lo[:, tile, :], sqr[:, m, :], u_hi[:, tile, :].bitcast(F32),
                                                ALU.subtract).then_inc(g_out, 1)

                def down(it, zs):
                    for z in zs:
                        lo_piece(e, n0 + it * 4 + (UP + z), z)
                        if z in (3, 5):
                            for m in range(2):
                                residual(e, it * 4 + (2 * (z // 5) + m), 4 * (z // 5) + 2 * m)
                if not last:
                    with e.Fori(0, DOWN_BLOCKS // 2) as it:
                        down(it, range(2, 6))
                else:
                    for it in range(DOWN_BLOCKS // 2 - 1):
                        down(it, range(2, 6))
                    down(DOWN_BLOCKS // 2 - 1, range(2, 4))
                    e.wait_ge(w_used, MLP0 + N_CHUNK * CHUNK_PIECES)
                    for m in range(2):
                        residual(e, KT - 2 + m, 4 + 2 * m)
            e.wait_ge(o_rstd, 1)
            with e.Fori(0, N_CHUNK - 1) as c:
                chunk(c, False)
            chunk(N_CHUNK - 1, True)

        y_0rdy, y_T, y_ev_a, y_ev_d, y_rs, y_col, y_ld = (
            sem(n) for n in ("y_0rdy", "y_T", "y_ev_a", "y_ev_d", "y_rs", "y_col", "y_ld"))
        G_LAST = G_MLP0 + (N_CHUNK - 1) * G_CHUNK + FC // P

        def final_act(e, blk):
            for k in (2 * blk, 2 * blk + 1):
                e.wait_ge(g_out, G_LAST + k + 1)
                e.wait_ge(o_sum, KT + k - 1)
                e.activation(sq2[:, k % 2, :], xf[:, k, :], ACT.Square).then_inc(o_sq, 1)
                e.activation(y_0[:, k, :], xf[:, k, :], ACT.Copy,
                             scale=pcol[:, R_LNFIN + k:R_LNFIN + k + 1]).then_inc(y_0rdy, 1)

        def final_pool(e):
            e.wait_ge(o_pe, 1)
            for k in range(KT):
                e.wait_ge(o_sq, KT + k + 1)
                if k == 0:
                    e.tensor_copy(ssq_a[:], sq2[:, 0, :]).then_inc(o_sum, 1)
                else:
                    e.wait_ge(o_sum, KT + k)
                    e.tensor_tensor(ssq_a[:], ssq_a[:], sq2[:, k % 2, :], ALU.add).then_inc(o_sum, 1)

        y_rms, y_rstd = small[:, 32:37], small[:, 40:45]

        Y_FILLS = [(t, q) for t in range(5) for q in range(4)]

        def y_src(t):
            return slice(t * P, t * P + P) if t < 4 else slice(SEQ, NT)

        def final_pe(e):
            e.wait_ge(g_out, G_LAST + KT)
            e.wait_ge(o_sum, 2 * KT)
            for t in range(5):
                n = P if t < 4 else NB
                last = e.matmul(PS[0:n, 7, t:t + 1], ssq_a[:, y_src(t)], ones[:, 0:1], start=True, stop=True)
            last.then_inc(y_rs, 1)
            e.wait_ge(y_0rdy, KT)
            for f, (t, q) in enumerate(Y_FILLS):
                n = P if t < 4 else NB
                if f >= 6:
                    e.wait_ge((y_ev_a, y_ev_d)[f % 2], f // 2 - 2)
                for x in range(4):
                    last = e.transpose(PS[0:n, f % 6, x * P:x * P + P], y_0[:, 4 * q + x, y_src(t)], ident[:])
                last.then_inc(y_T, 1)

        def final_out(e, par, copy, done):
            for f, (t, q) in enumerate(Y_FILLS):
                if f % 2 == par:
                    n = P if t < 4 else NB
                    dst = y_out[:, t, q * 512:q * 512 + 512] if t < 4 else ys_out[:, q * 512:q * 512 + 512]
                    e.wait_ge(y_T, f + 1)
                    copy(dst, PS[0:n, f % 6, :], y_rstd[0:n, t:t + 1]).then_inc(done, 1)

        def final_act2(e):
            e.wait_ge(y_rs, 1)
            e.activation(y_rms[:, 0:4], PS[:, 7, 0:4], ACT.Sqrt, scale=1.0 / D_MODEL, bias=eps_col[:]).then_inc(y_col, 1)
            e.activation(y_rms[0:NB, 4:5], PS[0:NB, 7, 4:5], ACT.Sqrt, scale=1.0 / D_MODEL,
                         bias=eps_col[0:NB, :]).then_inc(y_col, 1)
            e.wait_ge(y_ready, 2)
            final_out(e, 0, lambda a, b, s: e.activation(a, b, ACT.Copy, scale=s), y_ev_a)

        y_ready = sem("y_ready")

        def final_dve(e):
            e.wait_ge(y_col, 2)
            e.reciprocal(y_rstd[:, 0:4], y_rms[:, 0:4]).then_inc(y_ready, 1)
            e.reciprocal(y_rstd[0:NB, 4:5], y_rms[0:NB, 4:5]).then_inc(y_ready, 1)
            e.wait_ge(y_ready, 2)
            final_out(e, 1, lambda a, b, s: e.tensor_scalar(a, b, s, None, ALU.mult), y_ev_d)

        def final_sp(e):
            for t in range(5):
                e.wait_ge(y_ev_a, 2 * (t + 1))
                e.wait_ge(y_ev_d, 2 * (t + 1))
                if t < 4:
                    e.dma_start(o["y_prompt"][0, t * P:t * P + P, :], y_out[:, t, :]).then_inc(y_ld, 16)
                else:
                    e.dma_start(o["y_sample"].rearrange("b t d -> (b t) d"), ys_out[:]).then_inc(y_ld, 16)
            e.wait_ge(y_ld, 16 * 5)

        @block.sync
        def _(e):
            const_sp(e)
            x_sp(e)
            proj_sp(e)
            rows_sp(e)
            cmp_p_sp(e)
            values_sp(e)
            smp_sp(e)
            e.wait_ge(*n_mix(8))
            ssd_sp(e)
            out_sp(e)
            mlp_sp(e)
            final_sp(e)
            e.wait_ge(win_out, 16 * NB)

        @block.gpsimd
        def _(e):
            ch = Chain(e, pool_ch)
            const_pool(e, ch)
            compress_pool(e)
            const2_pool(e, ch)
            values_pool(e)
            q_pool(e)
            att_pool(e)
            smp_pool(e, ch)
            ssd_pool(e, ch)
            out_pool(e)
            final_pool(e)

        @block.scalar
        def _(e):
            ch = Chain(e, act_ch)
            compress_act(e)
            x_act(e, ch)
            proj_act(e, ch)
            rows_act(e)
            cmp_p_act(e)
            gate_act(e)
            att_cmp_act(e)
            att_act(e)
            smp_cmp_act(e)
            att_mix_act(e)
            smp_act(e)
            ssd_act(e, ch)
            ssd_end_act(e, ch)
            out_act(e)
            mlp_act(e)
            final_act2(e)

        @block.vector
        def _(e):
            ch = Chain(e, dve_ch)
            const_dve(e, ch)
            compress_dve(e)
            x_dve(e, ch)
            proj_dve(e, ch)
            rows_dve(e)
            cmp_p_dve(e)
            att_cmp_dve(e, ch)
            q_dve(e, ch)
            att_dve(e, ch)
            smp_dve(e, ch)
            ssd_dve(e, ch)
            ssd_end_dve(e, ch)
            out_dve(e, ch)
            mlp_dve(e)
            final_dve(e)

        @block.tensor
        def _(e):
            const_pe(e)
            compress_pe(e)
            x_pe(e)
            proj_pe(e)
            rows_pe(e)
            cmp_p_pe(e)
            gate_pe(e)
            att_cmp_pe(e)
            att_pe(e)
            smp_cmp_pe(e)
            att_mix_pe(e)
            smp_pe(e)
            ssd_pe(e)
            ssd_end_pe(e)
            out_pe(e)
            mlp_pe(e)
            final_pe(e)



INPUTS = ("x_prompt", "x_sample", "cache_kv_cmp", "cache_kv_sel", "state_kv_win", "state_conv", "state_ssm",
          "page_table", "ln_mix", "w_in", "cmp_pe", "cmp_w1", "cmp_b1", "cmp_w2", "cmp_b2", "conv_w", "conv_b",
          "dt_bias", "a_log", "d_skip", "ssm_norm", "w_out", "ln_mlp", "w_up", "w_down", "ln_final")
OUTPUTS = {
    "y_prompt": (1, SEQ, D_MODEL), "y_sample": (NB, 1, D_MODEL),
    "kv_cmp_p": (1, 1, SEQ, 2, NKV, HD), "kv_sel_p": (1, 1, SEQ, 2, NKV, HD),
    "kv_win_p": (1, 1, SEQ, 2, NKV, HD), "conv_p": (1, 1, 3, CONV_DIM), "ssm_p": (1, 1, NH, HD, DS),
    "kv_cmp_s": (1, NB, 1, 2, NKV, HD), "kv_sel_s": (1, NB, 1, 2, NKV, HD),
    "kv_win_s": (1, NB, WIN, 2, NKV, HD), "conv_s": (1, NB, 3, CONV_DIM), "ssm_s": (1, NB, NH, HD, DS),
}


def kernel(**inputs):
    import numpy as np
    import concourse.bacc as bacc
    from concourse.bass_utils import run_bass_kernel_spmd

    nc = bacc.Bacc("TRN2", target_bir_lowering=False, num_devices=1)
    arrays, ins, outs = {}, {}, {}
    for name in INPUTS:
        a = np.ascontiguousarray(inputs[name])
        arrays[f"in_{name}"] = a
        ins[name] = nc.dram_tensor(f"in_{name}", a.shape, mybir.dt.from_np(a.dtype), kind="ExternalInput").ap()
    for name, shape in OUTPUTS.items():
        outs[name] = nc.dram_tensor(f"out_{name}", shape, F32, kind="ExternalOutput").ap()
    build_program(nc, ins, outs)
    r = run_bass_kernel_spmd(nc, [arrays], core_ids=[0])
    return tuple(r.results[0][f"out_{name}"] for name in OUTPUTS)
```
